# Optimizing a Trainium2 kernel written in Bass

```python
import jax
import jax.numpy as jnp
from jax import lax
import numpy as np

'''Hybrid streaming-encoder trunk: DEPTH layers, each = [adaLN + sandwich-normed parallel token mixing (GLA | sliding-window GQA with sinks + ALiBi | HGRN2), sigmoid-gated merge] followed by [adaLN + sandwich-normed SwiGLU (even layers) / top-2-of-8 SwiGLU experts (odd layers)].
Inputs: x (BATCH, SEQ, D_MODEL) float32, c (BATCH, D_MODEL) float32 conditioning vector, plus per-layer parameters.
Output: (BATCH, SEQ, D_MODEL).'''

D_MODEL = 1024
BATCH = 1
SEQ = 256
DEPTH = 2

CHUNK = 64
EPS = 1e-6
NEG_LARGE = -1e30
N_MOD = 6
GLA_HEADS = 4
GLA_DK = 64
GLA_DV = 128
GLA_GATE_RANK = 16
GLA_GATE_NORMALIZER = 16.0
SWA_Q_HEADS = 8
SWA_KV_HEADS = 2
SWA_HEAD_DIM = 64
SWA_WINDOW_CHUNKS = 2
HGRN_HEADS = 4
HGRN_DK = 128
HGRN_DV = 128
N_BRANCHES = 3
BRANCH_WIDTH = 512
D_FF = 2816
N_EXPERTS = 8
TOP_K = 2
D_FF_EXPERT = 3584
MOE_BLOCK = 128
IN_SPLITS = (
    GLA_HEADS * GLA_DK, GLA_HEADS * GLA_DK, GLA_HEADS * GLA_DV, GLA_HEADS * GLA_DV, GLA_GATE_RANK,
    SWA_Q_HEADS * SWA_HEAD_DIM, SWA_KV_HEADS * SWA_HEAD_DIM, SWA_KV_HEADS * SWA_HEAD_DIM,
    HGRN_HEADS * HGRN_DK, HGRN_HEADS * HGRN_DK, HGRN_HEADS * HGRN_DV, HGRN_HEADS * HGRN_DV,
)
D_IN = sum(IN_SPLITS)

kernel_name = 'hybrid_gla_swa_hgrn2_moe_adaln'

def rms_norm(x, g):
    xf = x.astype(jnp.float32)
    y = xf * lax.rsqrt(jnp.mean(xf * xf, axis=-1, keepdims=True) + EPS)
    return (y * g.astype(jnp.float32)).astype(x.dtype)

def alibi_slopes(n):
    return 2.0 ** (-8.0 * jnp.arange(1, n + 1, dtype=jnp.float32) / n)

def chunk_gated_linear_attention(q, k, v, log_a):
    B_, S_, H, DK = q.shape
    DV = v.shape[-1]
    n_chunks = S_ // CHUNK

    def to_chunks(t):
        return t.reshape(B_, n_chunks, CHUNK, H, t.shape[-1]).transpose(1, 0, 3, 2, 4)

    causal = jnp.tril(jnp.ones((CHUNK, CHUNK), dtype=bool))[:, :, None]

    def step(state, inp):
        qi, ki, vi, ai = inp
        b = jnp.cumsum(ai, axis=-2)
        diff = b[..., :, None, :] - b[..., None, :, :]
        decay = jnp.where(causal, jnp.exp(jnp.where(causal, diff, 0.0)), 0.0)
        scores = jnp.einsum('bhtd,bhsd,bhtsd->bhts', qi, ki, decay)
        o = jnp.einsum('bhts,bhse->bhte', scores, vi) + jnp.einsum('bhtd,bhde->bhte', qi * jnp.exp(b), state)
        b_last = b[..., -1:, :]
        new_state = state * jnp.exp(b_last[..., 0, :])[..., None] + jnp.einsum('bhsd,bhse->bhde', ki * jnp.exp(b_last - b), vi)
        return new_state, o

    s0 = jnp.zeros((B_, H, DK, DV), jnp.float32)
    _, o = lax.scan(step, s0, (to_chunks(q), to_chunks(k), to_chunks(v), to_chunks(log_a)))
    return o.transpose(1, 0, 3, 2, 4).reshape(B_, S_, H, DV)

def sliding_window_attention(q, k, v, sinks):
    B_, S_, HQ, DH = q.shape
    HKV = k.shape[2]
    G = HQ // HKV
    n_chunks = S_ // CHUNK
    W = SWA_WINDOW_CHUNKS * CHUNK
    qb = q.reshape(B_, n_chunks, CHUNK, HKV, G, DH)

    def band(t):
        tc = t.reshape(B_, n_chunks, CHUNK, HKV, DH)
        parts = [jnp.pad(tc, ((0, 0), (j, 0), (0, 0), (0, 0), (0, 0)))[:, :n_chunks]
                 for j in range(SWA_WINDOW_CHUNKS - 1, -1, -1)]
        return jnp.concatenate(parts, axis=2)

    kb, vb = band(k), band(v)
    s = jnp.einsum('bnqhgd,bnkhd->bnhgqk', qb, kb).astype(jnp.float32) * (DH ** -0.5)
    q_pos = (SWA_WINDOW_CHUNKS - 1) * CHUNK + jnp.arange(CHUNK)
    k_pos = jnp.arange(W)
    dist = jnp.abs(q_pos[:, None] - k_pos[None, :]).astype(jnp.float32)
    s = s - alibi_slopes(HQ).reshape(HKV, G, 1, 1) * dist
    chunk_lag = (SWA_WINDOW_CHUNKS - 1) - k_pos // CHUNK
    valid = jnp.arange(n_chunks)[:, None] >= chunk_lag[None, :]
    s = jnp.where(valid[None, :, None, None, None, :], s, NEG_LARGE)
    sink = jnp.broadcast_to(sinks.astype(jnp.float32).reshape(HKV, G, 1, 1), s.shape[:-1] + (1,))
    p = jax.nn.softmax(jnp.concatenate([s, sink], axis=-1), axis=-1)[..., :W]
    o = jnp.einsum('bnhgqk,bnkhd->bnqhgd', p.astype(v.dtype), vb)
    return o.reshape(B_, S_, HQ * DH)

def token_mix(h, lb, w_in, gla_w_gate, gla_b_gate, gla_norm_g, swa_sinks, hgrn_norm_g, w_branch, w_merge, b_merge, w_out):
    B_, S_, _ = h.shape
    f32 = jnp.float32
    offsets = [int(o) for o in np.cumsum(IN_SPLITS)[:-1]]
    (gq, gk, gv, gg, glr, sq, sk, sv, hq, hf, hi, hg) = jnp.split(h @ w_in, offsets, axis=-1)

    def heads(t, n):
        return t.reshape(B_, S_, n, -1)

    log_a = jax.nn.log_sigmoid((glr @ gla_w_gate + gla_b_gate).astype(f32)) / GLA_GATE_NORMALIZER
    o_a = chunk_gated_linear_attention(heads(gq, GLA_HEADS).astype(f32) * (GLA_DK ** -0.5),
                                       heads(gk, GLA_HEADS).astype(f32),
                                       heads(gv, GLA_HEADS).astype(f32),
                                       heads(log_a, GLA_HEADS))
    o_a = (rms_norm(o_a, gla_norm_g) * jax.nn.silu(heads(gg, GLA_HEADS).astype(f32))).reshape(B_, S_, -1).astype(h.dtype)

    o_b = sliding_window_attention(heads(sq, SWA_Q_HEADS), heads(sk, SWA_KV_HEADS), heads(sv, SWA_KV_HEADS), swa_sinks).astype(h.dtype)

    f_raw = heads(hf, HGRN_HEADS).astype(f32)
    lb_h = lb.reshape(HGRN_HEADS, HGRN_DK)
    log_f = jax.nn.log_sigmoid(f_raw) + jnp.log1p(lb_h * jnp.exp(-f_raw))
    k_c = (1.0 - lb_h) * jax.nn.sigmoid(-f_raw)
    q_c = jax.nn.silu(heads(hq, HGRN_HEADS).astype(f32)) * (HGRN_DK ** -0.5)
    o_c = chunk_gated_linear_attention(q_c, k_c, heads(hi, HGRN_HEADS).astype(f32), log_f)
    o_c = (rms_norm(o_c, hgrn_norm_g) * jax.nn.silu(heads(hg, HGRN_HEADS).astype(f32))).reshape(B_, S_, -1).astype(h.dtype)

    gates = jax.nn.sigmoid((h @ w_merge + b_merge).astype(f32)).astype(h.dtype).reshape(B_, S_, N_BRANCHES, D_MODEL)
    merged = gates[:, :, 0] * (o_a @ w_branch[0])
    merged = merged + gates[:, :, 1] * (o_b @ w_branch[1])
    merged = merged + gates[:, :, 2] * (o_c @ w_branch[2])
    return merged @ w_out

def swiglu(h, w_gate, w_up, w_down):
    return (jax.nn.silu(h @ w_gate) * (h @ w_up)) @ w_down

def moe_swiglu(h, w_router, w_gate, w_up, w_down):
    B_, S_, D = h.shape
    N = B_ * S_
    A = N * TOP_K
    xs = h.reshape(N, D)
    logits = (xs @ w_router).astype(jnp.float32)
    top_logit, top_e = lax.top_k(logits, TOP_K)
    top_w = jax.nn.softmax(top_logit, axis=-1)
    e_flat = top_e.reshape(A)
    order = jnp.argsort(e_flat)
    e_sorted = e_flat[order]
    tok_sorted = (order // TOP_K).astype(jnp.int32)
    w_sorted = top_w.reshape(A)[order].astype(h.dtype)
    counts = jnp.zeros((N_EXPERTS,), jnp.int32).at[e_flat].add(1)
    padded = (counts + MOE_BLOCK - 1) // MOE_BLOCK * MOE_BLOCK
    pad_end = jnp.cumsum(padded)
    starts = jnp.cumsum(counts) - counts
    dest = (pad_end - padded)[e_sorted] + jnp.arange(A, dtype=jnp.int32) - starts[e_sorted]
    n_blocks = -(-A // MOE_BLOCK) + N_EXPERTS
    P = n_blocks * MOE_BLOCK
    tok_buf = jnp.zeros((P,), jnp.int32).at[dest].set(tok_sorted)
    w_buf = jnp.zeros((P,), h.dtype).at[dest].set(w_sorted)
    block_e = jnp.minimum(jnp.searchsorted(pad_end, jnp.arange(n_blocks, dtype=jnp.int32) * MOE_BLOCK, side='right'), N_EXPERTS - 1)

    def expert_block(args):
        idx, e = args
        xb = xs[idx]
        return (jax.nn.silu(xb @ w_gate[e]) * (xb @ w_up[e])) @ w_down[e]

    y = lax.map(expert_block, (tok_buf.reshape(n_blocks, MOE_BLOCK), block_e))
    y = y.reshape(P, D) * w_buf[:, None]
    return jnp.zeros((N, D), h.dtype).at[tok_buf].add(y).reshape(B_, S_, D)

def setup_inputs(seed: int = 0) -> dict:
    key = jax.random.key(seed)
    ks = jax.random.split(key, 24)
    f32 = jnp.float32
    n_dense = (DEPTH + 1) // 2
    n_moe = DEPTH // 2

    def nrm(k, shape, fan_in):
        return jax.random.normal(k, shape, f32) * (fan_in ** -0.5)

    def rnd(k, shape, scale):
        return jax.random.normal(k, shape, f32) * scale

    return {
        'x': jax.random.normal(ks[0], (BATCH, SEQ, D_MODEL), f32),
        'c': jax.random.normal(ks[1], (BATCH, D_MODEL), f32),
        'w_mod': nrm(ks[2], (DEPTH, D_MODEL, N_MOD * D_MODEL), D_MODEL) * 0.5,
        'b_mod': rnd(ks[3], (DEPTH, N_MOD * D_MODEL), 0.02),
        'norm_g': 1.0 + rnd(ks[4], (DEPTH, 4, D_MODEL), 0.05),
        'w_in': nrm(ks[5], (DEPTH, D_MODEL, D_IN), D_MODEL),
        'gla_w_gate': nrm(ks[6], (DEPTH, GLA_GATE_RANK, GLA_HEADS * GLA_DK), GLA_GATE_RANK),
        'gla_b_gate': rnd(ks[7], (DEPTH, GLA_HEADS * GLA_DK), 0.1),
        'gla_norm_g': 1.0 + rnd(ks[8], (DEPTH, GLA_DV), 0.05),
        'swa_sinks': rnd(ks[9], (DEPTH, SWA_Q_HEADS), 1.0),
        'hgrn_lb': rnd(ks[10], (DEPTH, HGRN_HEADS * HGRN_DK), 1.0),
        'hgrn_norm_g': 1.0 + rnd(ks[11], (DEPTH, HGRN_DV), 0.05),
        'w_branch': nrm(ks[12], (DEPTH, N_BRANCHES, BRANCH_WIDTH, D_MODEL), BRANCH_WIDTH),
        'w_merge': nrm(ks[13], (DEPTH, D_MODEL, N_BRANCHES * D_MODEL), D_MODEL),
        'b_merge': rnd(ks[14], (DEPTH, N_BRANCHES * D_MODEL), 0.1),
        'w_out': nrm(ks[15], (DEPTH, D_MODEL, D_MODEL), D_MODEL),
        'ffn_w_gate': nrm(ks[16], (n_dense, D_MODEL, D_FF), D_MODEL),
        'ffn_w_up': nrm(ks[17], (n_dense, D_MODEL, D_FF), D_MODEL),
        'ffn_w_down': nrm(ks[18], (n_dense, D_FF, D_MODEL), D_FF),
        'moe_router': nrm(ks[19], (n_moe, D_MODEL, N_EXPERTS), D_MODEL),
        'moe_w_gate': nrm(ks[20], (n_moe, N_EXPERTS, D_MODEL, D_FF_EXPERT), D_MODEL),
        'moe_w_up': nrm(ks[21], (n_moe, N_EXPERTS, D_MODEL, D_FF_EXPERT), D_MODEL),
        'moe_w_down': nrm(ks[22], (n_moe, N_EXPERTS, D_FF_EXPERT, D_MODEL), D_FF_EXPERT),
    }

def reference(x, c, w_mod, b_mod, norm_g, w_in, gla_w_gate, gla_b_gate, gla_norm_g, swa_sinks, hgrn_lb, hgrn_norm_g,
              w_branch, w_merge, b_merge, w_out, ffn_w_gate, ffn_w_up, ffn_w_down, moe_router, moe_w_gate, moe_w_up, moe_w_down):
    lb_soft = jax.nn.softmax(hgrn_lb.astype(jnp.float32), axis=0)
    lb_all = jnp.cumsum(lb_soft, axis=0) - lb_soft[0]
    mod = jnp.einsum('bd,lde->lbe', jax.nn.silu(c), w_mod) + b_mod[:, None, :]
    for l in range(DEPTH):
        sh_a, sc_a, g_a, sh_f, sc_f, g_f = jnp.split(mod[l][:, None, :], N_MOD, axis=-1)
        h = rms_norm(x, norm_g[l, 0]) * (1.0 + sc_a) + sh_a
        y = token_mix(h, lb_all[l], w_in[l], gla_w_gate[l], gla_b_gate[l], gla_norm_g[l], swa_sinks[l], hgrn_norm_g[l],
                      w_branch[l], w_merge[l], b_merge[l], w_out[l])
        x = x + g_a * rms_norm(y, norm_g[l, 1])
        h = rms_norm(x, norm_g[l, 2]) * (1.0 + sc_f) + sh_f
        if l % 2 == 0:
            y = swiglu(h, ffn_w_gate[l // 2], ffn_w_up[l // 2], ffn_w_down[l // 2])
        else:
            y = moe_swiglu(h, moe_router[l // 2], moe_w_gate[l // 2], moe_w_up[l // 2], moe_w_down[l // 2])
        x = x + g_f * rms_norm(y, norm_g[l, 3])
    return x


_drawn_inputs = setup_inputs


def setup_inputs(seed=0):
    import zlib

    import numpy as np

    out = dict(_drawn_inputs(seed))
    spreads = {}
    factors = {}
    for name, (base, spread) in spreads.items():
        noise = np.random.default_rng([zlib.crc32(name.encode()), seed]).standard_normal(out[name].shape)
        drawn = base * np.exp(spread * noise) if base else spread * noise
        out[name] = jnp.asarray(drawn.astype(out[name].dtype))
    for name, factor in factors.items():
        out[name] = (out[name] * factor).astype(out[name].dtype)
    return out
```

```python
from contextlib import ExitStack

import concourse.bass as bass
from concourse import mybir

F32 = mybir.dt.float32
F32R = mybir.dt.float32r
BF16 = mybir.dt.bfloat16
I32 = mybir.dt.int32
ALU = mybir.AluOpType
ACT = mybir.ActivationFunctionType
AX = mybir.AxisListType

P = 128
D = 1024
KD = D // P
SEQ = 256
NT = SEQ // P
DEPTH = 2
EPS = 1e-6
D_IN = 4368
D_FF = 2816
D_FFE = 3584
N_EXP = 8
ITEMS = 12
MAX_OVER = 3
FF = 256
N = 512
RING = 3

GQ, GK, GV, GG, GLR, SQ, SK, SV, HQ, HF, HI, HG = 0, 256, 512, 1024, 1536, 1552, 2064, 2192, 2320, 2832, 3344, 3856
W_IN_CHUNKS = [(HF, 512), (HQ, 512), (GQ, 512), (None, 272), (SQ, 512), (GV, 512), (HI, 512), (GG, 512), (HG, 512)]
N_WIN = len(W_IN_CHUNKS)
N_MERGE = 6
MIX_UNITS = 2 * (N_WIN + N_MERGE + 2) + 6
FFN_STEPS = D_FF // FF
MOE_STEPS = D_FFE // FF
U_FFN = MIX_UNITS
U_MIX1 = MIX_UNITS + 3 * FFN_STEPS
U_MOE = U_MIX1 + MIX_UNITS

R_BMOD, R_NORM, R_MERGE, N_ROWS = 0, 24, 40, 52

T_ID, T_ARG = 0, 128
T_F32 = 128 + 9 * 128
B_MASK, B_DIST, B_TRI, B_IOTA, B_ONES, B_ZERO = 0, 1024, 1408, 1536, 1664, 1792
T_BF16 = 1920
N_LEVELS = 7
NEVER = 1e33


class Chain:

    def __init__(self, eng, sem, base=0):
        self.eng, self.sem, self.n, self.base = eng, sem, 0, base

    def link(self, ins):
        self.n += 1
        ins.then_inc(self.sem, 1)
        self.eng.wait_ge(self.sem, self.base + self.n)


class Unit:

    def __init__(self, s, d=0):
        self.s, self.d, self.slot = s, d, s % RING
        self.number = 3 * d + s
        self.landed = 32 * (d + s // RING + 1)


def program(nc, a, out):
    with ExitStack() as ctx:
        def sb(name, shape, dt=F32):
            return ctx.enter_context(nc.sbuf_tensor(name, shape, dt))

        def sem(name):
            return ctx.enter_context(nc.semaphore(name))

        ring = sb("ring", [P, RING, 2048])
        w_hi = sb("w_hi", [P, RING, 2048], F32R)
        w_lo = sb("w_lo", [P, RING, 2048], F32R)
        x_hi = sb("x_hi", [P, KD * SEQ], F32R)
        x_lo = sb("x_lo", [P, KD * SEQ], F32R)
        a_hi = sb("a_hi", [P, 2 * SEQ], F32R)
        a_lo = sb("a_lo", [P, 2 * SEQ], F32R)
        r_hi = sb("r_hi", [P, KD * N_EXP], F32R)
        r_lo = sb("r_lo", [P, KD * N_EXP], F32R)
        tf = sb("tf", [P, T_F32])
        tb = sb("tb", [P, T_BF16], BF16)
        rows = sb("rows", [N_ROWS, N])
        row_cols = sb("row_cols", [P, 4, N_ROWS])
        ones = sb("ones", [P, 1])
        gate_w = sb("gate_w", [17, DEPTH, 256])
        glr_t = sb("glr_t", [17, SEQ])
        head_gain = sb("head_gain", [P, 2 * P])
        sinks = sb("sinks", [P, DEPTH * 8])
        c_rows = sb("c_rows", [KD, P])
        c_col = sb("c_col", [P, KD])
        mod_col = sb("mod_col", [P, DEPTH * 12, 4])
        s_col = sb("s_col", [P, KD])
        b_col = sb("b_col", [P, KD])
        col_tmp = sb("col_tmp", [P, 4])
        ssq = sb("ssq", [P, 16])
        var = sb("var", [P, 8])
        sd = sb("sd", [P, 8])
        rs = sb("rs", [P, 8])
        soft = sb("soft", [P, 8, 4])
        rden = sb("rden", [P, 2, 4])
        mem_words = 2048 + 2048 + 1024 * 2 + 544 + 256 + 4608 + 1536 + 4096 + 1024 + 4096 + 512
        mem = sb("mem", [P, mem_words])
        ids = sb("ids", [1, 4], I32)
        m_bf = sb("m_bf", [P, NT * N_EXP], BF16)
        at = [0]

        def carve(words):
            at[0] += words
            return mem[:, at[0] - words:at[0]]

        x = carve(2048)
        v_h, gate_h = x[:, 0:1024], x[:, 1024:2048]
        g_rows = carve(2048)
        v_g, gate_g = carve(1024), carve(1024)
        misc, sk_swap = carve(544), carve(256)
        ft = carve(4608)
        log_a, log_f = carve(512), carve(1024)
        gates = carve(4096)
        o_b = carve(1024)
        work = carve(4096)
        p_sum, p_cross, k_cross = carve(256), carve(128), carve(128)

        def tiles(ap, w):
            return ap.rearrange("p (t w) -> p t w", w=w)

        o_a, o_c, merged = ft[:, 0:1024], ft[:, 1536:2560], ft[:, 2560:4608]
        stage_f, stage_k, stage_q, stage_g = [gates[:, 1024 * i:1024 * i + 1024] for i in range(4)]
        xhat = gates[:, 0:2048]
        e_buf, q_buf, k_buf, p_buf = [work[:, 1024 * i:1024 * i + 1024] for i in range(4)]
        mod_ring = work[:, 0:2048].rearrange("p (s n) -> p s n", n=N)
        mod_acc = work[:, 2048:3072].rearrange("p (s n) -> p s n", n=N)
        lb_row, om_row = work[:, 3072:3584], work[:, 3584:4096]
        h_tmp = mem[:, at[0] - 512 - 4096 - 1024 - 4096 - 1536:][:, 0:1024].rearrange("p (b n) -> p b n", n=512)
        silu_buf, act_buf = v_g[:, 0:512], v_g[:, 512:1024]
        y_acc, y_sb, hg_tmp = ft[:, 0:2048], ft[:, 2048:3072], ft[:, 3072:4096]
        sel, sel_w, sel_t = gate_g[:, 0:256], gate_g[:, 256:512], gate_g[:, 512:768]
        cur = gate_g[:, 768:776]
        pos_items = gate_g[:, 776:776 + 2 * ITEMS].rearrange("p (i t) -> p i t", t=NT)
        w_items = gate_g[:, 800:800 + 2 * ITEMS].rearrange("p (i t) -> p i t", t=NT)
        r_raw = misc[:, 0:64]
        rt = work[:, 0:1024].rearrange("p (i n) -> p i n", n=16)

        ident = tf[:, T_ID:T_ID + P]
        ps = ctx.enter_context(nc.psum_tensor("ps", [P, 8, N], F32))

        def banks(i, k=1):
            return ps[:, i:i + k, :].rearrange("p b n -> p (b n)")

        s_const = sem("constants_landed")
        s_rows = sem("rows_landed")
        s_c = sem("c_landed")
        s_par = sem("head_parameters_landed")
        s_lb = sem("lower_bounds_landed")
        s_xin = sem("x_landed")
        s_xre = sem("x_back")
        s_gain = sem("head_gains_landed")
        s_park = sem("x_parked")
        s_router = sem("router_landed")
        s_unit = [sem(f"unit_landed{i}") for i in range(RING)]
        s_hi = sem("unit_hi")
        s_lo = sem("unit_lo")
        s_used = sem("unit_used")
        s_mod = [sem(f"mod_landed{i}") for i in range(4)]
        s_macc = sem("mod_accumulated")
        s_mps = sem("mod_summed")
        s_mev = sem("mod_taken")
        s_dch = sem("vector_chain")
        s_cols = sem("modulation_columns")
        s_ach = sem("scalar_chain")
        s_sq = sem("squares_summed")
        s_var = sem("variance_ready")
        s_sd = sem("deviation_ready")
        s_xhat = sem("xhat_ready")
        s_xupd = sem("x_updated")
        s_tr = sem("group_turned")
        s_tmp = sem("group_scaled")
        s_ghi = sem("group_hi")
        s_free = sem("group_taken")
        s_eva = sem("chunk_taken_scalar")
        s_evd = sem("chunk_taken_vector")
        s_kc = sem("sigmoid_ready")
        s_kr = sem("stage_k_ready")
        s_lbd = sem("bounds_shifted")
        s_lbe = sem("bounds_exp")
        s_f1 = sem("f_negated")
        s_f2 = sem("f_exponent")
        s_f3 = sem("f_bounded")
        s_f4 = sem("f_log_parts")
        s_logf = sem("log_f_ready")
        s_swap = sem("sk_swapped")
        s_glr = sem("glr_turned")
        s_la = sem("log_a_part")
        s_cs = sem("c_silu")
        s_ss = sem("swa_scores")
        s_sst = sem("swa_scores_taken")
        s_nm = sem("swa_max_ready")
        s_pr = sem("swa_probs")
        s_st = sem("swa_probs_turned")
        s_pt = sem("swa_turned_copied")
        s_so = sem("swa_out")
        s_soe = sem("swa_out_taken")
        s_arg = sem("decay_args")
        s_exp = sem("decay_exp")
        s_qe = sem("q_decayed")
        s_ke = sem("k_decayed")
        s_sc = sem("scan_scores")
        s_mask = sem("scan_masked")
        s_psum = sem("scan_summed")
        s_px = sem("scan_cross")
        s_o = sem("scan_out")
        s_oe = sem("scan_out_taken")
        s_heads = sem("heads_normed")
        s_merged = sem("merged_ready")
        s_fsilu = sem("ff_silu")
        s_fact = sem("ff_act")
        s_ftr = sem("ff_act_turned")
        s_fhi = sem("ff_act_hi")
        s_flo = sem("ff_act_lo")
        s_y = sem("y_taken")
        s_logit = sem("logits_ready")
        s_m = sem("choice_ready")
        s_pos = sem("positions_ready")
        s_top = sem("top_difference")
        s_tope = sem("top_exponent")
        s_rsp = sem("router_split")
        s_ids = sem("item_tables_ready")
        s_selw = sem("sel_w_ready")
        s_sel = sem("sel_ready")
        s_selt = sem("sel_turned")
        s_selc = sem("sel_t_ready")
        s_gat = sem("gathered")
        s_hg = sem("gathered_scaled")
        s_hghi = sem("gathered_hi")
        s_hglo = sem("gathered_lo")
        s_ysb = sem("y_copied")
        s_scat = sem("scattered")
        s_yadd = sem("y_added")
        s_mdch = sem("moe_vector_chain")
        s_out = sem("out_written")

        def w_src(ap, col, width, k0):
            return ap.rearrange("(k p) n -> p k n", p=P)[:, k0:k0 + 4, col:col + width]

        def load(sp, u, parts):
            if u.d is not 0 or u.s >= RING:
                sp.wait_ge(s_lo, u.number - (RING - 1))
            for dst, src in parts:
                sp.dma_start(dst, src).then_inc(s_unit[u.slot], 16)

        def load_plain(sp, u, ap, col, width, k0):
            dst = ring[:, u.slot, :].rearrange("p (k n) -> p k n", n=N)
            src = w_src(ap, col, width, k0)
            load(sp, u, [(dst[:, 0:2, 0:width], src[:, 0:2, :]), (dst[:, 2:4, 0:width], src[:, 2:4, :])])

        def load_misc(sp, u, ap, k0):
            dst = ring[:, u.slot, :].rearrange("p (k n) -> p k n", n=N)
            load(sp, u, [(dst[:, :, 0:16], w_src(ap, GLR, 16, k0)), (dst[:, :, 16:272], w_src(ap, SK, 256, k0))])

        def load_up(sp, u, gate, up, e, j, k0):
            dst = ring[:, u.slot, :].rearrange("p (k n) -> p k n", n=N)
            for half, w in ((0, gate), (1, up)):
                src = w.rearrange("e (k p) f -> e p k f", p=P)[bass.ds(e, 1), :, k0:k0 + 4, bass.ds(j * FF, FF)]
                if half == 0:
                    parts = []
                parts.append((dst[:, :, half * FF:half * FF + FF], src.rearrange("o p k f -> (o p) k f")))
            load(sp, u, parts)

        def load_down(sp, u, down, e, j):
            dst = ring[:, u.slot, :].rearrange("p (k n) -> p k n", n=D)
            view = down.rearrange("e (r p) n -> e p r n", p=P)
            parts = []
            for k in range(2):
                src = view[bass.ds(e, 1), :, bass.ds(j * 2 + k, 1), :]
                parts.append((dst[:, k, :], src.rearrange("o p k n -> (o p) (k n)")))
            load(sp, u, parts)

        def unit_view(buf, u, width):
            v = buf[:, u.slot, :]
            return v if width is None else v.rearrange("p (k n) -> p k n", n=N)[:, :, 0:width]

        def split_hi(act, u, width=None):
            act.wait_ge(s_unit[u.slot], u.landed)
            if u.d is not 0 or u.s >= RING:
                act.wait_ge(s_used, u.number - (RING - 1))
            nc.scalar.activation(unit_view(w_hi, u, width), unit_view(ring, u, width), ACT.Copy).then_inc(s_hi, 1)

        def split_lo(dve, u, width=None):
            dve.wait_ge(s_hi, u.number + 1)
            nc.vector.tensor_tensor(unit_view(w_lo, u, width), unit_view(ring, u, width),
                                    unit_view(w_hi, u, width).bitcast(F32), ALU.subtract).then_inc(s_lo, 1)

        def narrow(n):
            m = n if n < MIX_UNITS else n - U_MIX1
            return 272 if 0 <= m < 2 * N_WIN and W_IN_CHUNKS[m // 2][0] is None else None

        class Splits:

            def __init__(self, eng, split):
                self.eng, self.split, self.n = eng, split, 0

            def upto(self, n, end):
                while self.n < min(n, end):
                    self.split(self.eng, Unit(self.n), narrow(self.n))
                    self.n += 1

        def product(pe, u, left, acc, width, first, last, k0=0, groups=NT):
            wh = w_hi[:, u.slot, :].rearrange("p (k n) -> p k n", n=N)
            wl = w_lo[:, u.slot, :].rearrange("p (k n) -> p k n", n=N)
            pe.wait_ge(s_lo, u.number + 1)
            for k in range(4):
                for t in range(groups):
                    hi, lo = left(k0 + k, t)
                    for i, (l, r) in enumerate(((hi, wh), (hi, wl), (lo, wh))):
                        mm = nc.tensor.matmul(acc[t], l, r[:, k, 0:width], start=first and k == 0 and i == 0,
                                              stop=last and k == 3 and i == 2, skip_group_check=True)
            mm.then_inc(s_used, 1)

        def model_left(k, t):
            at = k * SEQ + t * P
            return x_hi[:, at:at + P], x_lo[:, at:at + P]

        G_LAYER = 4 + 11 + 6 + 4 + 4

        def group_bank(g):
            return banks(4 + g % 2)

        def swa_bank(h):
            return ps[:, 4 + h % 2, (h // 2) * 256:(h // 2) * 256 + 256]

        MOD_COLS1 = [0, 1, 2, 3, 6, 7, 8, 9]
        MOD = [(0, c) for c in range(12)] + [(1, c) for c in MOD_COLS1] + [(1, c) for c in (4, 5, 10, 11)]

        def mod_of_win(l, c):
            if l == 0:
                return 4 + c if c < 8 else None
            return 20 + c if c < 4 else None

        ARGS = [("G", p, t) for p in range(2) for t in range(NT)] + [("H", h, t) for h in range(4) for t in range(NT)]
        ROUNDS = [(i, j) for i, (kind, _, _) in enumerate(ARGS) for j in range(2 if kind == "G" else 1)]
        NA, NR = len(ARGS), len(ROUNDS)
        CROSS = [r for r, (i, _) in enumerate(ROUNDS) if ARGS[i][2] == 1]
        NX = len(CROSS)

        def rounds_before(i):
            return sum(1 for q, _ in ROUNDS if q < i)

        def cross_before(r):
            return sum(1 for q in CROSS if q < r)

        def rows_of(kind, j):
            return slice(64 * j, 64 * j + 64) if kind == "G" else slice(0, P)

        def ft_block(b, t=None):
            return ft[:, b * SEQ:b * SEQ + SEQ] if t is None else ft[:, b * SEQ + t * P:b * SEQ + t * P + P]

        def q_block(kind, i, t):
            return ft_block((6 if kind == "G" else 10) + i, t)

        def k_block(kind, i, t):
            return ft_block((8 if kind == "G" else 14) + i, t)

        def merge_gate(m, t):
            buf = gates[:, m * 1024:m * 1024 + 1024] if m < 4 else (v_g if m == 4 else e_buf)
            return buf[:, t * N:t * N + N]

        def pair(c):
            if c < N_WIN:
                return 2 * (c % 2)
            return 0 if c < 15 else 2 * ((c - 15) % 2)

        BRANCHES = [1, 0, 2]

        block = ctx.enter_context(nc.Block())

        @block.sync
        def _(sp):
            def mix_units(l, base):
                u = base
                for col, width in W_IN_CHUNKS:
                    for k0 in (0, 4):
                        if col is None:
                            load_misc(sp, Unit(u), a["w_in"][l], k0)
                        else:
                            load_plain(sp, Unit(u), a["w_in"][l], col, width, k0)
                        u += 1
                for m in range(N_MERGE):
                    for k0 in (0, 4):
                        load_plain(sp, Unit(u), a["w_merge"][l], m * N, N, k0)
                        u += 1
                for b in BRANCHES:
                    for n in range(2):
                        load_plain(sp, Unit(u), a["w_branch"][l, b], n * N, N, 0)
                        u += 1
                for n in range(2):
                    for k0 in (0, 4):
                        load_plain(sp, Unit(u), a["w_out"][l], n * N, N, k0)
                        u += 1

            def ff_units(base, d0, gate, up, down, e, steps):
                load_up(sp, Unit(base, d0), gate, up, e, 0, 0)
                load_up(sp, Unit(base + 1, d0), gate, up, e, 0, 4)
                with sp.Fori(0, steps - 1) as i:
                    load_up(sp, Unit(base + 2, d0 + i), gate, up, e, i + 1, 0)
                    load_up(sp, Unit(base + 3, d0 + i), gate, up, e, i + 1, 4)
                    load_down(sp, Unit(base + 4, d0 + i), down, e, i)
                load_down(sp, Unit(base + 2, d0 + (steps - 1)), down, e, steps - 1)

            sp.dma_start(c_rows[:], a["c"].rearrange("b (k p) -> (b k) p", p=P)).then_inc(s_c, 16)
            sp.dma_start(tf[:], a["table_f32"]).then_inc(s_const, 16)
            sp.dma_start(rows[0:24, :], a["b_mod"].rearrange("l (c n) -> (l c) n", n=N)).then_inc(s_rows, 16)
            sp.dma_start(rows[24:40, :], a["norm_g"].rearrange("l i (h n) -> (l i h) n", n=N)).then_inc(s_rows, 16)
            sp.dma_start(rows[40:52, :], a["b_merge"].rearrange("l (m n) -> (l m) n", n=N)).then_inc(s_rows, 16)
            sp.dma_start(x.rearrange("p (t d) -> p t d", d=D), a["x"].rearrange("b (t p) d -> (b p) t d", p=P)) \
                .then_inc(s_xin, 16)
            sp.dma_start(tb[:], a["table_bf16"]).then_inc(s_const, 16)
            sp.dma_start(gate_w[0:16, :, :], a["gla_w_gate"].rearrange("l r n -> r l n")).then_inc(s_par, 16)
            sp.dma_start(gate_w[16:17, :, :], a["gla_b_gate"].rearrange("l n -> (l n)").unsqueeze(0)
                         .rearrange("o (l n) -> o l n", n=256)).then_inc(s_par, 16)
            sp.dma_start(glr_t[16:17, :], a["ones_row"]).then_inc(s_par, 16)
            sp.dma_start(sinks[:], a["swa_sinks"].rearrange("l h -> (l h)").unsqueeze(0).to_broadcast([P, 16])) \
                .then_inc(s_par, 16)
            sp.wait_ge(s_macc, 16)
            mix_units(0, 0)
            ff_units(U_FFN, 0, a["ffn_w_gate"], a["ffn_w_up"], a["ffn_w_down"], 0, FFN_STEPS)
            mix_units(1, U_MIX1)
            wg, wu, wd = [a[n].rearrange("o e k n -> (o e) k n") for n in ("moe_w_gate", "moe_w_up", "moe_w_down")]
            with sp.Fori(0, N_EXP) as e:
                ff_units(U_MOE, e * MOE_STEPS, wg, wu, wd, e, MOE_STEPS)
            sp.wait_ge(s_ids, 1)
            over = sp.value_load(ids[0:1, 0:1], min_val=0, max_val=MAX_OVER)
            with sp.If(over > 0):
                with sp.Fori(0, over) as r:
                    e = sp.value_load(ids[0:1, bass.ds(r + 1, 1)], min_val=0, max_val=N_EXP - 1)
                    ff_units(U_MOE, (r + N_EXP) * MOE_STEPS, wg, wu, wd, e, MOE_STEPS)
            sp.wait_ge(s_xupd, 2 * 2 * NT)
            sp.dma_start(out.rearrange("b (t p) d -> (b p) t d", p=P), x.rearrange("p (t d) -> p t d", d=D)) \
                .then_inc(s_out, 16)
            sp.wait_ge(s_out, 16)
            sp.wait_ge(s_park, 16)

        @block.gpsimd
        def _(pool):
            def mod_load(q, l, col, first=False):
                for k in range(KD):
                    s = k % 4
                    if not (first and k < 4):
                        pool.wait_ge(s_macc, 8 * q + (k - 3))
                    pool.dma_start(mod_ring[:, s, :], a["w_mod"][l, k * P:k * P + P, bass.ds(col, N)]) \
                        .then_inc(s_mod[s], 16)

            nc.gpsimd.memset(ones[:], 1.0).then_inc(s_const, 1)
            for q in range(4):
                mod_load(q, 0, q * N, first=(q == 0))
            for l in range(DEPTH):
                if l == 1:
                    pool.wait_ge(s_heads, 2)
                for i, name in enumerate(("gla_norm_g", "hgrn_norm_g")):
                    pool.dma_start(head_gain[:, i * P:i * P + P], a[name][l:l + 1, :].to_broadcast([P, P])) \
                        .then_inc(s_gain, 16)
                if l == 1:
                    pool.wait_ge(s_sd, 6 + 1)
                    pool.dma_start(o_b, a["hgrn_lb"].rearrange("l n -> (l n)").unsqueeze(0).to_broadcast([P, 1024])) \
                        .then_inc(s_lb, 16)
                for c in range(N_WIN):
                    q = mod_of_win(l, c)
                    if q is not None:
                        mod_load(q, l, MOD[q][1] * N)
                for i, (kind, n, t) in enumerate(ARGS):
                    pool.wait_ge(s_exp, l * NA + i + 1)
                    if i == 0:
                        pool.wait_ge(s_free, l * G_LAYER + 16)
                        pool.wait_ge(s_so, 4 * l + 4)
                    else:
                        pool.wait_ge(s_sc, l * NR + rounds_before(i))
                    ev = e_buf.rearrange("p (v n) -> p v n", n=P)
                    kv = k_buf.rearrange("p (v n) -> p v n", n=P)
                    key = k_block(kind, n, t)
                    if t == 0:
                        nc.gpsimd.tensor_tensor(k_cross, ev[:, 7, :], key, ALU.mult)
                    nc.gpsimd.tensor_tensor(kv[:, t:t + 7, :], ev[:, t:t + 7, :],
                                            key[:, None, :].to_broadcast([P, 7, P]), ALU.mult).then_inc(s_ke, 1)
                pool.wait_ge(s_heads, 2 * l + 2)
                if l == 1:
                    pool.wait_ge(s_park, 16)
                src = a["x"] if l == 0 else out
                pool.dma_start(x.rearrange("p (t d) -> p t d", d=D), src.rearrange("b (t p) d -> (b p) t d", p=P)) \
                    .then_inc(s_xre, 16)
                if l == 0:
                    pool.wait_ge(s_evd, 12)
                    with pool.Fori(0, 8) as i:
                        mod_load(i + 12, 1, i * N + (i // 4) * (2 * N))
                    pool.wait_ge(s_xupd, 2 * NT)
                    pool.dma_start(out.rearrange("b (t p) d -> (b p) t d", p=P), x.rearrange("p (t d) -> p t d", d=D)) \
                        .then_inc(s_park, 16)
                if l == 1:
                    pool.wait_ge(s_evd, 24)
                    pool.dma_start(r_raw.rearrange("p (k e) -> p k e", e=N_EXP),
                                   a["moe_router"].rearrange("o (k p) e -> (o p) k e", p=P)).then_inc(s_router, 16)

        @block.scalar
        def _(act):
            ch = Chain(act, s_ach)
            sp_ = Splits(act, split_hi)

            def deviation(n, width=2):
                act.wait_ge(s_var, n + 1)
                nc.scalar.activation(sd[:, 0:width], var[:, 0:width], ACT.Sqrt).then_inc(s_sd, 1)

            def group_hi(src, dst):
                nc.scalar.activation(dst, src, ACT.Copy).then_inc(s_ghi, 1)

            squares = [0]

            def square(src, t, dst=None):
                if squares[0]:
                    act.wait_ge(s_sq, squares[0])
                nc.scalar.activation(o_b if dst is None else dst, src, ACT.Square, accum_out=ssq[:, t:t + 1]) \
                    .then_inc(s_sq, 1)
                squares[0] += 1

            def norm(n, r):
                for t in range(NT):
                    square(x[:, t * D:t * D + D], t)
                deviation(r)
                for i in range(4):
                    act.wait_ge(s_tmp, 4 * n + i + 1)
                    group_hi(h_tmp[:, i % 2, :], x_hi[:, i * 512:i * 512 + 512])

            def copy(dst, src, scale=1.0, fn=ACT.Copy):
                return nc.scalar.activation(dst, src, fn, scale=scale)

            def ff(base, d0, f0, steps, nt):
                def silu(j, used):
                    act.wait_ge(s_used, used)
                    act.wait_ge(s_fact, f0 + j)
                    nc.scalar.activation(silu_buf.rearrange("p (t n) -> p t n", n=FF)[:, 0:nt, :], ps[:, 0:nt, 0:FF],
                                         ACT.Silu).then_inc(s_fsilu, 1)

                def act_hi(j):
                    act.wait_ge(s_ftr, f0 + j + 1)
                    w = 2 * nt * P
                    nc.scalar.activation(a_hi[:, 0:w], banks(2)[:, 0:w], ACT.Copy).then_inc(s_fhi, 1)

                def step(j, used):
                    split_hi(act, Unit(base + 2, d0 + j))
                    silu(j, used)
                    split_hi(act, Unit(base + 3, d0 + j))
                    act_hi(j)
                    split_hi(act, Unit(base + 4, d0 + j))

                split_hi(act, Unit(base, d0))
                split_hi(act, Unit(base + 1, d0))
                step(0, Unit(base + 2, d0).number)
                with act.Fori(1, steps - 1) as j:
                    step(j, Unit(base + 1, d0 + j).number)
                last = steps - 1
                silu(last, Unit(base + 1, d0 + last).number)
                act_hi(last)
                split_hi(act, Unit(base + 2, d0 + last))

            act.wait_ge(s_tr, 1)
            nc.scalar.activation(c_col[:], banks(4)[:, 0:KD], ACT.Silu).then_inc(s_cs, 1)
            for l in range(DEPTH):
                base = l * U_MIX1
                end = base + MIX_UNITS
                g_layer = 2 + l * G_LAYER
                sp_.n = base

                if l == 0:
                    act.wait_ge(s_xin, 16)
                else:
                    act.wait_ge(s_xupd, 2 * NT)
                sp_.upto(base + 2, end)
                norm(2 * l, 6 * l)
                if l == 1:
                    act.wait_ge(s_lbd, 1)
                    nc.scalar.activation(o_b, o_b, ACT.Exp).then_inc(s_lbe, 1)
                    act.wait_ge(s_park, 16)

                def evac_win(c):
                    act.wait_ge(s_used, base + 2 * c + 2)
                    if c == 1:
                        act.wait_ge(s_tr, g_layer + 4)
                    for t in range(NT):
                        src = ps[:, pair(c) + t, :]
                        w = slice(t * N, t * N + N)
                        if c == 0:
                            ins = copy(stage_f[:, w], src)
                        elif c == 1:
                            ins = copy(stage_q[:, w], src, fn=ACT.Silu)
                        elif c == 2:
                            copy(stage_g[:, t * N:t * N + 256], src[:, 0:256], scale=0.125)
                            ins = copy(stage_g[:, t * N + 256:t * N + 512], src[:, 256:512])
                        elif c == 3:
                            ins = copy(misc[:, t * 272:t * 272 + 272], src[:, 0:272])
                        elif c == 4:
                            if t == 0:
                                act.wait_ge(s_logf, l + 1)
                            ins = copy(stage_f[:, w], src, scale=0.125)
                        elif c == 5:
                            ins = copy(v_g[:, w], src)
                        elif c == 6:
                            ins = copy(v_h[:, w], src)
                        elif c == 7:
                            ins = copy(gate_g[:, w], src, fn=ACT.Silu)
                        else:
                            ins = copy(gate_h[:, w], src, fn=ACT.Silu)
                        ins.then_inc(s_eva, 1)

                for c in range(N_WIN + 1):
                    if c > 0:
                        evac_win(c - 1)
                    if c == 1:
                        act.wait_ge(s_xhat, (2 * l + 1) * NT)
                        act.wait_ge(s_eva, 30 * l + 2)
                        nc.scalar.activation(stage_k, stage_f, ACT.Sigmoid, scale=-1.0).then_inc(s_kc, 1)
                        ch.link(nc.scalar.activation(gate_h, stage_f, ACT.Abs))
                        ch.link(nc.scalar.activation(gate_h, gate_h, ACT.Exp, scale=-1.0))
                        nc.scalar.activation(gate_h, gate_h, ACT.Ln, bias=1.0).then_inc(s_f4, 1)
                    if c == 2:
                        act.wait_ge(s_f1, l + 1)
                        nc.scalar.activation(gate_g, gate_g, ACT.Exp).then_inc(s_f2, 1)
                    if c == 3:
                        act.wait_ge(s_f3, l + 1)
                        nc.scalar.activation(gate_g, gate_g, ACT.Ln, bias=1.0).then_inc(s_f4, 1)
                    if c == 4:
                        act.wait_ge(s_eva, 30 * l + 8)
                        for t in range(NT):
                            m = t * 272
                            copy(sk_swap[:, t * P:t * P + 64], misc[:, m + 80:m + 144]).then_inc(s_swap, 1)
                            copy(sk_swap[:, t * P + 64:t * P + P], misc[:, m + 16:m + 80]).then_inc(s_swap, 1)
                    if c == 6:
                        g = g_layer + 4 + 10
                        act.wait_ge(s_tr, g + 1)
                        z = stage_q[:, 0:512]
                        ch.link(nc.scalar.activation(z, group_bank(g), ACT.Abs))
                        ch.link(nc.scalar.activation(z, z, ACT.Exp, scale=-1.0))
                        nc.scalar.activation(z, z, ACT.Ln, bias=1.0).then_inc(s_la, 1)
                    sp_.upto(base + 2 * c + 4, end)

                def swa_exp(i):
                    w = P * (i % 2 + 1)
                    act.wait_ge(s_nm, 4 * l + i + 1)
                    for h in range(4):
                        nc.scalar.activation(q_buf[:, h * 256:h * 256 + w], e_buf[:, h * 256:h * 256 + w], ACT.Exp,
                                             bias=soft[:, 1, h:h + 1], accum_out=soft[:, 3, h:h + 1])
                    nc.scalar.activation(soft[:, 4, :], soft[:, 2, :], ACT.Exp).then_inc(s_pr, 1)

                def merge_done(k):
                    if k % 2 == 0:
                        return
                    m = k // 2
                    act.wait_ge(s_used, base + 2 * (N_WIN + m) + 2)
                    if m == 0:
                        act.wait_ge(s_free, g_layer + 14)
                    if m == 4:
                        act.wait_ge(s_o, NR * l + 8)
                    if m == 5:
                        act.wait_ge(s_qe, NA * l + NA)
                        act.wait_ge(s_ke, NA * l + NA)
                    for t in range(NT):
                        nc.scalar.activation(merge_gate(m, t), ps[:, t, :], ACT.Sigmoid).then_inc(s_eva, 1)

                swa_exp(0)
                for i in range(4):
                    act.wait_ge(s_st, 4 * l + i + 1)
                    if i > 0:
                        act.wait_ge(s_so, 4 * l + i)
                    nb = 4 * (i % 2 + 1)
                    nc.scalar.activation(k_buf[:, 0:nb * P], banks(6, 2)[:, 0:nb * P], ACT.Copy).then_inc(s_pt, 1)
                    merge_done(i)
                    sp_.upto(base + 2 * N_WIN + i + 4, end)
                    if i < 3:
                        swa_exp(i + 1)

                def decay(i):
                    act.wait_ge(s_arg, NA * l + i + 1)
                    if i > 0:
                        act.wait_ge(s_qe, NA * l + i)
                        act.wait_ge(s_ke, NA * l + i)
                    nc.scalar.activation(e_buf, banks(4, 2), ACT.Exp).then_inc(s_exp, 1)

                def out_taken(r):
                    i, j = ROUNDS[r]
                    kind, n, t = ARGS[i]
                    act.wait_ge(s_o, NR * l + r + 1)
                    head = 2 * n + j if kind == "G" else n
                    dst = (o_a if kind == "G" else o_c)[:, t * N + head * P:t * N + head * P + P]
                    nc.scalar.activation(dst, banks(3)[:, (r % 2) * P:(r % 2) * P + P], ACT.Copy).then_inc(s_oe, 1)

                decay(0)
                for i in range(NA):
                    for r in [r for r, (q, _) in enumerate(ROUNDS) if q == i]:
                        if r > 0:
                            out_taken(r - 1)
                        if ROUNDS[r][1] == 0 and i + 1 < NA:
                            decay(i + 1)
                        if ARGS[i][2] == 1:
                            act.wait_ge(s_sc, NR * l + r + 1)
                            nc.scalar.activation(p_cross, banks(2)[:, 0:P], ACT.Copy).then_inc(s_px, 1)
                    if i < 7:
                        merge_done(4 + i)
                        sp_.upto(base + 2 * N_WIN + 4 + i + 4, end)
                out_taken(NR - 1)
                merge_done(11)

                def branch_hi(bi):
                    g = g_layer + 15 + 2 * bi
                    for i in range(2):
                        act.wait_ge(s_tr, g + i + 1)
                        at = (bi % 2) * 1024 + i * 512
                        group_hi(group_bank(g + i), x_hi[:, at:at + 512])

                branch_hi(0)
                sp_.upto(base + 30 + 3, end)
                deviation(6 * l + 1, 8)
                branch_hi(1)
                sp_.upto(base + 32 + 3, end)
                deviation(6 * l + 2, 8)
                branch_hi(2)
                sp_.upto(base + 34 + 3, end)
                for i in range(4):
                    g = g_layer + 21 + i
                    act.wait_ge(s_tr, g + 1)
                    group_hi(group_bank(g), x_hi[:, i * 512:i * 512 + 512])
                sp_.upto(end, end)
                act.wait_ge(s_used, end)
                for t in range(NT):
                    square(ps[:, t:4:2, :], t, o_b.rearrange("p (a n) -> p a n", n=N))
                deviation(6 * l + 3)
                act.wait_ge(s_xupd, (2 * l + 1) * NT)
                norm(2 * l + 1, 6 * l + 4)
                if l == 0:
                    ff(U_FFN, 0, 0, FFN_STEPS, NT)
                    act.wait_ge(s_used, U_MIX1)
                    for t in range(NT):
                        square(banks(4 + 2 * t, 2), t)
                    deviation(5)

            act.wait_ge(s_router, 16)
            nc.scalar.activation(r_hi[:], r_raw, ACT.Copy).then_inc(s_rsp, 1)
            act.wait_ge(s_top, 1)
            nc.scalar.activation(rt[:, 8, 2:4], rt[:, 8, 0:2], ACT.Exp).then_inc(s_tope, 1)

            def hg_hi(n):
                act.wait_ge(s_hg, n)
                nc.scalar.activation(x_hi[:, 0:1024], hg_tmp, ACT.Copy).then_inc(s_hghi, 1)

            act.wait_ge(s_ids, 1)
            items = act.value_load(ids[0:1, 0:1], min_val=0, max_val=MAX_OVER) + N_EXP
            hg_hi(1)
            with act.Fori(0, items) as it:
                act.wait_ge(s_selt, it + 1)
                nc.scalar.activation(sel_t, banks(3)[:, 0:2 * P], ACT.Copy).then_inc(s_selc, 1)
                ff(U_MOE, it * MOE_STEPS, it * MOE_STEPS + FFN_STEPS, MOE_STEPS, 1)
                hg_hi(it + 2)
                act.wait_ge(s_used, Unit(U_MOE, (it + 1) * MOE_STEPS).number)
                nc.scalar.activation(y_sb, banks(4, 2), ACT.Copy).then_inc(s_ysb, 1)
            act.wait_ge(s_yadd, items * 2)
            for t in range(NT):
                square(y_acc[:, t * D:t * D + D], t)
            deviation(11)

        @block.vector
        def _(dve):
            ch = Chain(dve, s_dch)
            sp_ = Splits(dve, split_lo)
            v = nc.vector

            def mod_acc_chunk(q):
                if not (isinstance(q, int) and q == 0):
                    dve.wait_ge(s_mps, q)
                acc = mod_acc[:, 0, :]
                for k in range(KD):
                    s = k % 4
                    dve.wait_ge(s_mod[s], 16 * (2 * q + k // 4 + 1))
                    if k == 0:
                        v.tensor_scalar(acc, mod_ring[:, s, :], c_col[:, 0:1], None, ALU.mult).then_inc(s_macc, 1)
                    else:
                        dve.wait_ge(s_macc, 8 * q + k)
                        v.scalar_tensor_tensor(out=acc, in0=mod_ring[:, s, :], scalar=c_col[:, k:k + 1], in1=acc,
                                               op0=ALU.mult, op1=ALU.add).then_inc(s_macc, 1)

            def mod_take_col(q, index, bank=6):
                dve.wait_ge(s_mps, q + 1)
                v.tensor_copy(index, banks(bank)[:, 0:4].rearrange("p (o j) -> p o j", o=1)).then_inc(s_mev, 1)

            def mod_take(q):
                l, c = MOD[q]
                if c in (4, 5, 10, 11):
                    at = (c // 6) * D + (c % 2) * N
                    dve.wait_ge(s_mps, q + 1)
                    ch.link(v.tensor_copy(g_rows[:, at:at + N], banks(7)))
                    v.tensor_tensor(g_rows[:, at:at + N], banks(6), g_rows[:, at:at + N], ALU.mult).then_inc(s_mev, 1)
                else:
                    mod_take_col(q, mod_col[:, l * 12 + c:l * 12 + c + 1, :])

            def columns(l, which, taken):
                dve.wait_ge(s_mev, taken)
                for half in range(2):
                    sc, sh = l * 12 + 6 * which + 2 + half, l * 12 + 6 * which + half
                    gain = R_NORM + (l * 4 + 2 * which) * 2 + half
                    j = slice(4 * half, 4 * half + 4)
                    ch.link(v.tensor_tensor(col_tmp[:], mod_col[:, sc, :], row_cols[:, :, sc], ALU.add))
                    ch.link(v.scalar_tensor_tensor(out=s_col[:, j], in0=col_tmp[:], scalar=1.0,
                                                   in1=row_cols[:, :, gain], op0=ALU.add, op1=ALU.mult))
                    ch.link(v.tensor_tensor(b_col[:, j], mod_col[:, sh, :], row_cols[:, :, sh], ALU.add))

            def rstd(r, squares, n, width):
                if squares:
                    dve.wait_ge(s_sq, squares)
                v.tensor_scalar(var[:, 0:n], ssq[:, 0:n], 1.0 / width, EPS, ALU.mult, ALU.add).then_inc(s_var, 1)
                dve.wait_ge(s_sd, r + 1)
                ch.link(v.reciprocal(rs[:, 0:n], sd[:, 0:n]))

            def norm(n, g0):
                for t in range(NT):
                    v.tensor_scalar(xhat[:, t * D:t * D + D], x[:, t * D:t * D + D], rs[:, t:t + 1], None, ALU.mult) \
                        .then_inc(s_xhat, 1)

                def scaled(i):
                    dve.wait_ge(s_tr, g0 + i + 1)
                    for k in range(2):
                        ins = v.tensor_scalar(h_tmp[:, i % 2, k * SEQ:k * SEQ + SEQ],
                                              group_bank(g0 + i)[:, k * SEQ:k * SEQ + SEQ],
                                              s_col[:, 2 * i + k:2 * i + k + 1], b_col[:, 2 * i + k:2 * i + k + 1],
                                              ALU.mult, ALU.add)
                    ins.then_inc(s_tmp, 1)

                def low(i):
                    dve.wait_ge(s_tmp, 4 * n + i + 1)
                    hi = 18 * (n // 2) + (0 if n % 2 == 0 else 14) + i + 1
                    dve.wait_ge(s_ghi, hi)
                    w = slice(i * 512, i * 512 + 512)
                    v.tensor_tensor(x_lo[:, w], h_tmp[:, i % 2, :], x_hi[:, w].bitcast(F32), ALU.subtract) \
                        .then_inc(s_free, 1)

                scaled(0)
                scaled(1)
                low(0)
                scaled(2)
                low(1)
                scaled(3)
                low(2)
                low(3)

            def residual(n, y):
                gr = g_rows[:, (n % 2) * D:(n % 2) * D + D]
                for t in range(NT):
                    src = y(t)
                    if len(src.shape) == 3:
                        tmp, g3 = o_b.rearrange("p (a n) -> p a n", n=N), gr.rearrange("p (a n) -> p a n", n=N)
                    else:
                        tmp, g3 = o_b, gr
                    if t:
                        dve.wait_ge(s_xupd, NT * n + t)
                    ch.link(v.scalar_tensor_tensor(out=tmp, in0=src, scalar=rs[:, t:t + 1], in1=g3,
                                                   op0=ALU.mult, op1=ALU.mult))
                    xt = x[:, t * D:t * D + D]
                    v.tensor_tensor(xt, xt, o_b, ALU.add).then_inc(s_xupd, 1)

            def ff(base, d0, f0, steps, nt, before=None, after=None, mod_steps=0):
                def mult(j):
                    dve.wait_ge(s_fsilu, f0 + j + 1)
                    s3 = silu_buf.rearrange("p (t n) -> p t n", n=FF)[:, 0:nt, :]
                    a3 = act_buf.rearrange("p (t n) -> p t n", n=FF)[:, 0:nt, :]
                    v.tensor_tensor(a3, s3, ps[:, 0:nt, FF:2 * FF], ALU.mult).then_inc(s_fact, 1)

                def act_lo(j):
                    dve.wait_ge(s_fhi, f0 + j + 1)
                    w = 2 * nt * P
                    v.tensor_tensor(a_lo[:, 0:w], banks(2)[:, 0:w], a_hi[:, 0:w].bitcast(F32), ALU.subtract) \
                        .then_inc(s_flo, 1)

                def step(j):
                    split_lo(dve, Unit(base + 2, d0 + j))
                    mult(j)
                    split_lo(dve, Unit(base + 3, d0 + j))
                    act_lo(j)
                    split_lo(dve, Unit(base + 4, d0 + j))

                split_lo(dve, Unit(base, d0))
                split_lo(dve, Unit(base + 1, d0))
                if mod_steps:
                    with dve.Fori(0, mod_steps) as j:
                        mod_acc_chunk(j + 12)
                        step(j)
                        mod_take_col(j + 12, mod_col[:, bass.ds(j + (j // 4) * 2 + 12, 1), :], 3)
                    with dve.Fori(mod_steps, steps - 1) as j:
                        step(j)
                else:
                    with dve.Fori(0, steps - 1) as j:
                        step(j)
                last = steps - 1
                mult(last)
                act_lo(last)
                split_lo(dve, Unit(base + 2, d0 + last))

            dve.wait_ge(s_tr, 2)
            v.tensor_copy(row_cols[:].rearrange("p j r -> p (j r)"), banks(5)[:, 0:4 * N_ROWS]).then_inc(s_free, 1)
            dve.wait_ge(s_cs, 1)
            dve.wait_ge(s_free, 1)
            for q in range(4):
                mod_acc_chunk(q)
                mod_take(q)

            for l in range(DEPTH):
                base = l * U_MIX1
                end = base + MIX_UNITS
                g_layer = 2 + l * G_LAYER
                gw = g_layer + 4
                sp_.n = base
                hi0 = 18 * l

                columns(l, 0, 4 if l == 0 else 20)
                sp_.upto(base + 2, end)
                rstd(6 * l, 8 * l + 2, 2, D)
                norm(2 * l, g_layer)

                if l == 0:
                    ch.link(v.memset(lb_row, 0.0))
                    ch.link(v.memset(om_row, float(P) ** -0.5))
                else:
                    dve.wait_ge(s_lb, 16)
                    ch.link(v.tensor_tensor(lb_row, o_b[:, 0:512], o_b[:, 512:1024], ALU.max))
                    ob3 = o_b.rearrange("p (l n) -> p l n", n=512)
                    v.tensor_tensor(ob3, ob3, lb_row[:, None, :].to_broadcast([P, 2, 512]), ALU.subtract) \
                        .then_inc(s_lbd, 1)
                    dve.wait_ge(s_lbe, 1)
                    ch.link(v.tensor_tensor(om_row, o_b[:, 0:512], o_b[:, 512:1024], ALU.add))
                    ch.link(v.reciprocal(om_row, om_row))
                    ch.link(v.tensor_tensor(lb_row, o_b[:, 512:1024], om_row, ALU.mult))
                    ch.link(v.tensor_scalar(om_row, lb_row, -1.0, 1.0, ALU.mult, ALU.add))
                    ch.link(v.tensor_scalar(om_row, om_row, float(P) ** -0.5, None, ALU.mult))
                lb3 = lb_row[:, None, :].to_broadcast([P, NT, 512])
                om3 = om_row[:, None, :].to_broadcast([P, NT, 512])

                def t3(ap):
                    return ap.rearrange("p (t n) -> p t n", t=NT)

                def take_group(i, block):
                    dve.wait_ge(s_tr, gw + i + 1)
                    v.tensor_copy(ft[:, block * SEQ:block * SEQ + 512], group_bank(gw + i)).then_inc(s_free, 1)

                for c in range(N_WIN + 1):
                    if c == 1:
                        dve.wait_ge(s_eva, 30 * l + 2)
                        if l == 1:
                            dve.wait_ge(s_park, 16)
                        v.tensor_scalar(gate_g, stage_f, -1.0, 40.0, ALU.mult, ALU.min).then_inc(s_f1, 1)
                    if c == 2:
                        dve.wait_ge(s_kc, l + 1)
                        v.tensor_tensor(t3(stage_k), t3(stage_k), om3, ALU.mult).then_inc(s_kr, 1)
                        dve.wait_ge(s_f2, l + 1)
                        v.tensor_tensor(t3(gate_g), t3(gate_g), lb3, ALU.mult).then_inc(s_f3, 1)
                    if c == 3:
                        take_group(0, 10)
                        take_group(1, 12)
                        dve.wait_ge(s_f4, 2 * l + 2)
                        ch.link(v.scalar_tensor_tensor(out=log_f, in0=stage_f, scalar=0.0, in1=gate_h,
                                                       op0=ALU.min, op1=ALU.subtract))
                        ch.link(v.tensor_tensor(log_f, log_f, gate_g, ALU.add))
                        ch.link(v.tensor_scalar(v_h, stage_f, 40.0, 0.0, ALU.add, ALU.min))
                        ch.link(v.scalar_tensor_tensor(out=t3(v_h), in0=lb3, scalar=0.0, in1=t3(v_h),
                                                       op0=ALU.is_gt, op1=ALU.mult))
                        v.tensor_tensor(log_f, log_f, v_h, ALU.subtract).then_inc(s_logf, 1)
                    if c == 4:
                        take_group(2, 14)
                        take_group(3, 16)
                        take_group(4, 6)
                        take_group(5, 8)
                    if c == 5:
                        dve.wait_ge(s_tr, gw + 7)
                        v.tensor_copy(glr_t[0:16, :], group_bank(gw + 6)[0:16, 0:SEQ]).then_inc(s_free, 1)
                        take_group(7, 4)
                    if c == 6:
                        take_group(8, 0)
                        take_group(9, 2)
                        dve.wait_ge(s_tr, gw + 11)
                        dve.wait_ge(s_la, l + 1)
                        ch.link(v.scalar_tensor_tensor(out=log_a, in0=group_bank(gw + 10), scalar=0.0,
                                                       in1=stage_q[:, 0:512], op0=ALU.min, op1=ALU.subtract))
                        v.tensor_scalar(log_a, log_a, 1.0 / 16.0, None, ALU.mult).then_inc(s_free, 1)
                    q = mod_of_win(l, c - 1)
                    if c > 0 and q is not None:
                        mod_take(q)
                    sp_.upto(base + 2 * c + 4, end)
                    q = mod_of_win(l, c) if c < N_WIN else None
                    if q is not None:
                        mod_acc_chunk(q)

                dve.wait_ge(s_par, 16 * 4)
                dve.wait_ge(s_gain, 32 * (l + 1))

                def swa_max(i):
                    g, t = i // 2, i % 2
                    w = P * (t + 1)
                    dve.wait_ge(s_ss, 4 * l + i + 1)
                    dist = tb[:, B_DIST + P * t:B_DIST + P * t + w]
                    for h in range(4):
                        slope = 2.0 ** -(4 * g + h + 1)
                        ins = v.scalar_tensor_tensor(out=e_buf[:, h * 256:h * 256 + w], in0=dist, scalar=-slope,
                                                     in1=swa_bank(h)[:, 0:w], op0=ALU.mult, op1=ALU.add)
                    ins.then_inc(s_sst, 1)
                    dve.wait_ge(s_sst, 4 * l + i + 1)
                    sink = sinks[:, l * 8 + 4 * g:l * 8 + 4 * g + 4]
                    ch.link(v.tensor_reduce(soft[:, 0, :], e_buf.rearrange("p (h w) -> p h w", w=256)[:, :, 0:w],
                                            AX.X, ALU.max))
                    ch.link(v.tensor_tensor(soft[:, 0, :], soft[:, 0, :], sink, ALU.max))
                    ch.link(v.tensor_scalar(soft[:, 1, :], soft[:, 0, :], -1.0, None, ALU.mult))
                    v.tensor_tensor(soft[:, 2, :], sink, soft[:, 0, :], ALU.subtract).then_inc(s_nm, 1)

                def swa_taken(i):
                    g, t = i // 2, i % 2
                    dve.wait_ge(s_so, 4 * l + i + 1)
                    for h in range(4):
                        at = t * N + (4 * g + h) * 64
                        ins = v.tensor_scalar(o_b[:, at:at + 64], banks(3)[:, h * 64:h * 64 + 64],
                                              rden[:, i % 2, h:h + 1], None, ALU.mult)
                    ins.then_inc(s_soe, 1)

                swa_max(0)
                for i in range(4):
                    dve.wait_ge(s_pr, 4 * l + i + 1)
                    ch.link(v.tensor_tensor(soft[:, 5, :], soft[:, 3, :], soft[:, 4, :], ALU.add))
                    ch.link(v.reciprocal(rden[:, i % 2, :], soft[:, 5, :]))
                    if i < 3:
                        swa_max(i + 1)
                    sp_.upto(base + 2 * N_WIN + i + 4, end)
                    swa_taken(i)

                def queries(i):
                    kind, n, t = ARGS[i]
                    dve.wait_ge(s_exp, NA * l + i + 1)
                    if i > 0:
                        dve.wait_ge(s_sc, NR * l + rounds_before(i))
                    lv = 7 + t
                    ev = e_buf.rearrange("p (v n) -> p v n", n=P)[:, 0:lv, :]
                    qv = q_buf.rearrange("p (v n) -> p v n", n=P)[:, 0:lv, :]
                    v.tensor_tensor(qv, ev, q_block(kind, n, t)[:, None, :].to_broadcast([P, lv, P]), ALU.mult) \
                        .then_inc(s_qe, 1)

                def mask_sum(r):
                    dve.wait_ge(s_sc, NR * l + r + 1)
                    if r > 0:
                        dve.wait_ge(s_psum, NR * l + r)
                    v.tensor_tensor(p_buf, banks(6, 2), tb[:, B_MASK:B_MASK + 1024], ALU.mult).then_inc(s_mask, 1)
                    dve.wait_ge(s_mask, NR * l + r + 1)
                    if r > 1:
                        dve.wait_ge(s_o, NR * l + r - 1)
                    v.tensor_reduce(p_sum[:, (r % 2) * P:(r % 2) * P + P], p_buf.rearrange("p (v n) -> p n v", n=P),
                                    AX.X, ALU.add).then_inc(s_psum, 1)

                queries(0)
                for i in range(NA):
                    for r in [r for r, (q, _) in enumerate(ROUNDS) if q == i]:
                        mask_sum(r)
                    if i + 1 < NA:
                        queries(i + 1)
                    if i < 7:
                        sp_.upto(base + 2 * N_WIN + 4 + i + 4, end)

                def low_group(g, hi, at):
                    dve.wait_ge(s_ghi, hi0 + hi + 1)
                    v.tensor_tensor(x_lo[:, at:at + 512], group_bank(g), x_hi[:, at:at + 512].bitcast(F32),
                                    ALU.subtract).then_inc(s_free, 1)

                def branch_low(bi):
                    for i in range(2):
                        low_group(g_layer + 15 + 2 * bi + i, 4 + 2 * bi + i, (bi % 2) * 1024 + i * 512)

                def heads(o, gate, which):
                    dve.wait_ge(s_oe, NR * l + NR)
                    o3 = o.rearrange("p (b e) -> p b e", e=P)
                    ch.link(v.tensor_tensor(p_buf, o, o, ALU.mult))
                    ch.link(v.tensor_reduce(ssq[:, 0:8], p_buf.rearrange("p (b e) -> p b e", e=P), AX.X, ALU.add))
                    rstd(6 * l + 1 + which, 0, 8, P)
                    gain = head_gain[:, which * P:which * P + P]
                    ch.link(v.tensor_tensor(o3, o3, rs[:, 0:8][:, :, None].to_broadcast([P, 8, P]), ALU.mult))
                    ch.link(v.tensor_tensor(o3, o3, gain[:, None, :].to_broadcast([P, 8, P]), ALU.mult))
                    v.tensor_tensor(o, o, gate, ALU.mult).then_inc(s_heads, 1)

                def gated(bi):
                    b = BRANCHES[bi]
                    for n in range(2):
                        c = 15 + 2 * bi + n
                        dve.wait_ge(s_used, base + 30 + 2 * bi + n + 1)
                        if bi == 0 and n == 0:
                            dve.wait_ge(s_eva, 30 * l + 30)
                        for t in range(NT):
                            m = merged[:, t * D + n * N:t * D + n * N + N]
                            src = ps[:, pair(c) + t, :]
                            gate = merge_gate(2 * b + n, t)
                            if bi == 0:
                                v.tensor_tensor(m, src, gate, ALU.mult).then_inc(s_evd, 1)
                            else:
                                tmp = p_buf[:, t * N:t * N + N]
                                v.tensor_tensor(tmp, src, gate, ALU.mult).then_inc(s_evd, 1)
                                dve.wait_ge(s_evd, 12 * l + 4 * bi + 2 * n + t + 1)
                                ins = v.tensor_tensor(m, m, tmp, ALU.add)
                                if bi == 2:
                                    ins.then_inc(s_merged, 1)
                                else:
                                    ch.link(ins)

                branch_low(0)
                sp_.upto(base + 30 + 3, end)
                heads(o_a, gate_g, 0)
                branch_low(1)
                gated(0)
                sp_.upto(base + 32 + 3, end)
                heads(o_c, gate_h, 1)
                branch_low(2)
                gated(1)
                sp_.upto(base + 34 + 3, end)
                gated(2)
                for i in range(4):
                    low_group(g_layer + 21 + i, 10 + i, i * 512)
                sp_.upto(end, end)
                rstd(6 * l + 3, 8 * l + 4, 2, D)
                dve.wait_ge(s_xre, 16 * (l + 1))
                residual(2 * l, lambda t: ps[:, t:4:2, :])
                columns(l, 1, 10 if l == 0 else 20)
                rstd(6 * l + 4, 8 * l + 6, 2, D)
                norm(2 * l + 1, g_layer + 25)
                if l == 0:
                    ff(U_FFN, 0, 0, FFN_STEPS, NT, mod_steps=8)
                    rstd(5, 8, 2, D)
                    residual(1, lambda t: banks(4 + 2 * t, 2))

            dve.wait_ge(s_rsp, 1)
            v.tensor_tensor(r_lo[:], r_raw, r_hi[:].bitcast(F32), ALU.subtract).then_inc(s_rsp, 1)
            ch.link(v.memset(y_acc, 0.0))
            lg, eq, one1, lg2, one2, wsel, mem_, pos_m = [rt[:, i, :].rearrange("p (t e) -> p t e", e=N_EXP) for i in range(8)]
            small = rt[:, 9, :]
            rev = rt[:, 10, 0:8]
            over, rank, hot = rt[:, 10, 8:16], rt[:, 11, 0:8], rt[:, 11, 8:16]
            prod = rt[:, 12, 0:8]
            idf = rt[:, 13, 0:4]
            iota = tb[:, B_IOTA:B_IOTA + P]

            def bc(col):
                return col[:, :, None].to_broadcast([P, NT, N_EXP])

            ch.link(v.tensor_scalar(rev, iota[:, 0:8], -1.0, 8.0, ALU.mult, ALU.add))
            dve.wait_ge(s_logit, 1)
            ch.link(v.tensor_copy(rt[:, 0, :], banks(6)[:, 0:16]))

            def choose(src, one, m):
                ch.link(v.tensor_reduce(small[:, m:m + 2], src, AX.X, ALU.max))
                ch.link(v.tensor_tensor(eq, src, bc(small[:, m:m + 2]), ALU.is_equal))
                ch.link(v.tensor_tensor(eq, eq, rev[:, None, :].to_broadcast([P, NT, N_EXP]), ALU.mult))
                ch.link(v.tensor_reduce(small[:, 4:6], eq, AX.X, ALU.max))
                ch.link(v.tensor_tensor(one, eq, bc(small[:, 4:6]), ALU.is_equal))

            choose(lg, one1, 0)
            ch.link(v.scalar_tensor_tensor(out=rt[:, 3, :], in0=rt[:, 2, :], scalar=-3.0e38, in1=rt[:, 0, :],
                                           op0=ALU.mult, op1=ALU.add))
            choose(lg2, one2, 2)
            ch.link(v.tensor_tensor(rt[:, 6, :], rt[:, 2, :], rt[:, 4, :], ALU.add))
            v.tensor_copy(m_bf[:], rt[:, 6, :]).then_inc(s_m, 1)
            v.tensor_tensor(rt[:, 8, 0:2], small[:, 2:4], small[:, 0:2], ALU.subtract).then_inc(s_top, 1)
            dve.wait_ge(s_tope, 1)
            ch.link(v.tensor_scalar(small[:, 6:8], rt[:, 8, 2:4], 1.0, None, ALU.add))
            ch.link(v.reciprocal(small[:, 8:10], small[:, 6:8]))
            ch.link(v.tensor_tensor(small[:, 10:12], small[:, 8:10], rt[:, 8, 2:4], ALU.mult))
            ch.link(v.tensor_tensor(one1, one1, bc(small[:, 8:10]), ALU.mult))
            ch.link(v.tensor_tensor(one2, one2, bc(small[:, 10:12]), ALU.mult))
            ch.link(v.tensor_tensor(wsel, one1, one2, ALU.add))
            dve.wait_ge(s_pos, 1)
            ch.link(v.tensor_scalar(rt[:, 7, :], banks(7)[:, 0:16], 1.0, None, ALU.add))
            ch.link(v.tensor_tensor(rt[:, 7, :], rt[:, 7, :], rt[:, 6, :], ALU.mult))
            ch.link(v.tensor_scalar(rt[:, 7, :], rt[:, 7, :], -1.0, None, ALU.add))
            ch.link(v.memset(gate_g[:, 776:824], 0.0))
            for t in range(NT):
                ch.link(v.tensor_copy(pos_items[:, 0:8, t], pos_m[:, t, :]))
                ch.link(v.tensor_copy(w_items[:, 0:8, t], wsel[:, t, :]))
            ch.link(v.tensor_scalar(over, banks(7)[:, 16:24], float(P), None, ALU.is_gt))
            ch.link(v.memset(rank[:, 0:1], 0.0))
            for e in range(1, N_EXP):
                ch.link(v.tensor_tensor(rank[:, e:e + 1], rank[:, e - 1:e], over[:, e - 1:e], ALU.add))
            ch.link(v.tensor_tensor(idf[:, 0:1], rank[:, 7:8], over[:, 7:8], ALU.add))
            ch.link(v.tensor_scalar(rt[:, 7, :], rt[:, 7, :], -float(P), None, ALU.add))
            for r in range(MAX_OVER):
                ch.link(v.scalar_tensor_tensor(out=hot, in0=rank, scalar=float(r), in1=over,
                                               op0=ALU.is_equal, op1=ALU.mult))
                ch.link(v.tensor_tensor(prod, hot, iota[:, 0:8], ALU.mult))
                ch.link(v.tensor_reduce(idf[:, r + 1:r + 2], prod, AX.X, ALU.add))
                for t in range(NT):
                    ch.link(v.tensor_tensor(prod, hot, pos_m[:, t, :], ALU.mult))
                    ch.link(v.tensor_reduce(pos_items[:, 8 + r, t:t + 1], prod, AX.X, ALU.add))
                    ch.link(v.tensor_tensor(prod, hot, wsel[:, t, :], ALU.mult))
                    ch.link(v.tensor_reduce(w_items[:, 8 + r, t:t + 1], prod, AX.X, ALU.add))
            v.tensor_copy(ids[:], idf[0:1, :]).then_inc(s_ids, 1)

            mch = Chain(dve, s_mdch)

            def current(i):
                mch.link(v.tensor_copy(cur[:, 0:2].rearrange("p (o t) -> p o t", o=1), pos_items[:, bass.ds(i, 1), :]))
                mch.link(v.tensor_copy(cur[:, 2:4].rearrange("p (o t) -> p o t", o=1), w_items[:, bass.ds(i, 1), :]))

            def select():
                for t in range(NT):
                    ins = v.tensor_scalar(sel[:, t * P:t * P + P], iota, cur[:, t:t + 1], None, ALU.is_equal)
                ins.then_inc(s_sel, 1)

            def gathered(n):
                dve.wait_ge(s_gat, n)
                for k in range(KD):
                    ins = v.tensor_scalar(hg_tmp[:, k * P:k * P + P], banks(6, 2)[:, k * P:k * P + P],
                                          s_col[:, k:k + 1], b_col[:, k:k + 1], ALU.mult, ALU.add)
                ins.then_inc(s_hg, 1)
                dve.wait_ge(s_hghi, n)
                v.tensor_tensor(x_lo[:, 0:1024], hg_tmp, x_hi[:, 0:1024].bitcast(F32), ALU.subtract) \
                    .then_inc(s_hglo, 1)

            dve.wait_ge(s_ids, 1)
            items = dve.value_load(ids[0:1, 0:1], min_val=0, max_val=MAX_OVER) + N_EXP
            current(0)
            select()
            gathered(1)
            with dve.Fori(0, items) as it:
                mch.base = it * 2
                for t in range(NT):
                    ins = v.tensor_scalar(sel_w[:, t * P:t * P + P], iota, cur[:, t:t + 1], cur[:, 2 + t:3 + t],
                                          ALU.is_equal, ALU.mult)
                ins.then_inc(s_selw, 1)
                dve.wait_ge(s_selw, it + 1)
                current(it + 1)
                select()
                ff(U_MOE, it * MOE_STEPS, it * MOE_STEPS + FFN_STEPS, MOE_STEPS, 1)
                gathered(it + 2)
                for t in range(NT):
                    dve.wait_ge(s_scat, 2 * it + t + 1)
                    v.tensor_tensor(y_acc[:, t * D:t * D + D], y_acc[:, t * D:t * D + D], banks(6 - 2 * t, 2), ALU.add) \
                        .then_inc(s_yadd, 1)
            rstd(11, 16, 2, D)
            residual(3, lambda t: y_acc[:, t * D:t * D + D])

        @block.tensor
        def _(pe):
            t_ = nc.tensor

            def row(r):
                return ident[0:N_ROWS, r:r + 1].to_broadcast([N_ROWS, P])

            def mod_sum_col(q, bank=6):
                pe.wait_ge(s_macc, 8 * q + 8)
                if not (isinstance(q, int) and q == 0):
                    pe.wait_ge(s_mev, q)
                for j in range(4):
                    mm = t_.matmul(banks(bank)[:, j:j + 1], mod_acc[:, 0, j * P:j * P + P], ones[:], start=True, stop=True)
                mm.then_inc(s_mps, 1)

            def mod_sum(q):
                l, c = MOD[q]
                if c not in (4, 5, 10, 11):
                    mod_sum_col(q)
                    return
                pe.wait_ge(s_mev, q)
                gain = R_NORM + (l * 4 + (1 if c < 6 else 3)) * 2 + c % 2
                t_.matmul(banks(7), row(gain), rows[:], start=True, stop=True)
                t_.matmul(banks(6), row(R_BMOD + 12 * l + c), rows[:], start=True, stop=False)
                pe.wait_ge(s_macc, 8 * q + 8)
                t_.matmul(banks(6), ones[:].to_broadcast([P, P]), mod_acc[:, 0, :], start=False, stop=True) \
                    .then_inc(s_mps, 1)

            def turn_group(g, blocks):
                if g >= 3:
                    pe.wait_ge(s_free, g - 2)
                for i, src in enumerate(blocks):
                    mm = t_.transpose(group_bank(g)[:, i * P:i * P + P], src, ident)
                mm.then_inc(s_tr, 1)

            def norm_groups(n, g0):
                pe.wait_ge(s_xhat, (n + 1) * NT)
                for i in range(4):
                    turn_group(g0 + i, [xhat[:, t * D + k * P:t * D + k * P + P] for k in (2 * i, 2 * i + 1)
                                        for t in range(NT)])

            def stage_groups(g, stage, width=N):
                for i in range(width // 256):
                    turn_group(g + i, [stage[:, t * N + k * P:t * N + k * P + P] for k in (2 * i, 2 * i + 1)
                                       for t in range(NT)])

            def ff(base, d0, f0, steps, nt, left, last_hook=None, mod_steps=0):
                def up(j, u0, u1):
                    pe.wait_ge(s_fact, f0 + j)
                    acc = [ps[:, t, :] for t in range(nt)]
                    product(pe, u0, left, acc, N, True, False, 0, nt)
                    product(pe, u1, left, acc, N, False, True, 4, nt)

                def turn(j):
                    pe.wait_ge(s_fact, f0 + j + 1)
                    pe.wait_ge(s_flo, f0 + j)
                    for k in range(2):
                        for t in range(nt):
                            at = (k * nt + t) * P
                            mm = t_.transpose(banks(2)[:, at:at + P], act_buf[:, t * FF + k * P:t * FF + k * P + P], ident)
                    mm.then_inc(s_ftr, 1)

                def down(j, u):
                    pe.wait_ge(s_flo, f0 + j + 1)
                    pe.wait_ge(s_lo, u.number + 1)
                    wh = w_hi[:, u.slot, :].rearrange("p (k n) -> p k n", n=D)
                    wl = w_lo[:, u.slot, :].rearrange("p (k n) -> p k n", n=D)
                    for k in range(2):
                        for t in range(nt):
                            at = (k * nt + t) * P
                            hi, lo = a_hi[:, at:at + P], a_lo[:, at:at + P]
                            for n in range(2):
                                for lhs, rhs in ((hi, wh), (hi, wl), (lo, wh)):
                                    mm = t_.matmul(ps[:, 4 + 2 * t + n, :], lhs, rhs[:, k, n * N:n * N + N],
                                                   start=False, stop=False, skip_group_check=True)
                    mm.then_inc(s_used, 1)

                for b in range(4, 4 + 2 * nt):
                    t_.matmul(ps[:, b, :], tb[:, B_ZERO:B_ZERO + P], tb[:, B_MASK:B_MASK + N], start=True, stop=False,
                              skip_group_check=True)
                up(0, Unit(base, d0), Unit(base + 1, d0))
                turn(0)

                def step(j):
                    up(j + 1, Unit(base + 2, d0 + j), Unit(base + 3, d0 + j))
                    down(j, Unit(base + 4, d0 + j))
                    turn(j + 1)

                if mod_steps:
                    with pe.Fori(0, mod_steps) as j:
                        mod_sum_col(j + 12, 3)
                        step(j)
                    with pe.Fori(mod_steps, steps - 1) as j:
                        step(j)
                else:
                    with pe.Fori(0, steps - 1) as j:
                        step(j)
                if last_hook:
                    last_hook()
                down(steps - 1, Unit(base + 2, d0 + (steps - 1)))

            pe.wait_ge(s_const, 33)
            pe.wait_ge(s_c, 16)
            t_.transpose(banks(4)[:, 0:KD], c_rows[:], ident[0:KD, 0:KD]).then_inc(s_tr, 1)
            pe.wait_ge(s_rows, 48)
            for j in range(4):
                mm = t_.transpose(banks(5)[:, j * N_ROWS:j * N_ROWS + N_ROWS], rows[:, j * P:j * P + P],
                                  ident[0:N_ROWS, 0:N_ROWS])
            mm.then_inc(s_tr, 1)
            for q in range(4):
                mod_sum(q)

            for l in range(DEPTH):
                base = l * U_MIX1
                g_layer = 2 + l * G_LAYER
                gw = g_layer + 4
                if l == 0:
                    pe.wait_ge(s_cs, 1)
                norm_groups(2 * l, g_layer)
                pe.wait_ge(s_free, g_layer - 1 + 4)

                for c in range(N_WIN):
                    if c >= 2:
                        pe.wait_ge(s_eva, 30 * l + 2 * (c - 1))
                    width = W_IN_CHUNKS[c][1]
                    acc = [ps[:, pair(c) + t, 0:width] for t in range(NT)]
                    product(pe, Unit(base + 2 * c), model_left, acc, width, True, False, 0)
                    product(pe, Unit(base + 2 * c + 1), model_left, acc, width, False, True, 4)
                    if c == 2:
                        pe.wait_ge(s_eva, 30 * l + 4)
                        stage_groups(gw, stage_q)
                    if c == 3:
                        pe.wait_ge(s_kr, l + 1)
                        stage_groups(gw + 2, stage_k)
                        pe.wait_ge(s_eva, 30 * l + 6)
                        stage_groups(gw + 4, stage_g)
                    if c == 4:
                        pe.wait_ge(s_eva, 30 * l + 8)
                        pe.wait_ge(s_free, gw + 6 - 2)
                        for t in range(NT):
                            mm = t_.transpose(group_bank(gw + 6)[0:16, t * P:t * P + P], misc[:, t * 272:t * 272 + 16], ident)
                        mm.then_inc(s_tr, 1)
                        pe.wait_ge(s_swap, 4 * l + 4)
                        turn_group(gw + 7, [misc[:, t * 272 + 16:t * 272 + 144] for t in range(NT)] +
                                   [sk_swap[:, t * P:t * P + P] for t in range(NT)])
                    if c == 5:
                        pe.wait_ge(s_eva, 30 * l + 10)
                        stage_groups(gw + 8, stage_f)
                        if l == 0:
                            pe.wait_ge(s_par, 16 * 4)
                        pe.wait_ge(s_free, gw + 10 - 2)
                        for t in range(NT):
                            mm = t_.matmul(group_bank(gw + 10)[:, t * 256:t * 256 + 256], glr_t[:, t * P:t * P + P],
                                           gate_w[:, l, :], start=True, stop=True)
                        mm.then_inc(s_tr, 1)
                    q = mod_of_win(l, c)
                    if q is not None:
                        mod_sum(q)

                def merge(k):
                    m = k // 2
                    if k % 2 == 0:
                        pe.wait_ge(s_eva, 30 * l + 2 * (N_WIN + m))
                        for t in range(NT):
                            t_.matmul(ps[:, t, :], row(R_MERGE + 6 * l + m), rows[:], start=True, stop=False,
                                      skip_group_check=True)
                    product(pe, Unit(base + 2 * N_WIN + k), model_left, [ps[:, t, :] for t in range(NT)], N,
                            False, k % 2 == 1, 4 * (k % 2))

                def swa_scores(i):
                    g, t = i // 2, i % 2
                    if i == 0:
                        pe.wait_ge(s_free, gw + 10)
                        pe.wait_ge(s_mev, 12 if l == 0 else 24)
                    else:
                        pe.wait_ge(s_sst, 4 * l + i)
                    for h in range(4):
                        half = slice(64 * (h % 2), 64 * (h % 2) + 64)
                        q = ft_block((4 * g + h) // 2, t)[half, :]
                        k = ft_block(4 if h % 2 == g else 5)[half, 0:P * (t + 1)]
                        mm = t_.matmul(swa_bank(h)[:, 0:P * (t + 1)], q, k, start=True, stop=True)
                    mm.then_inc(s_ss, 1)

                def swa_turn(i):
                    t = i % 2
                    pe.wait_ge(s_pr, 4 * l + i + 1)
                    if i > 0:
                        pe.wait_ge(s_pt, 4 * l + i)
                    for h in range(4):
                        for kb in range(t + 1):
                            at = (h * (t + 1) + kb) * P
                            mm = t_.transpose(banks(6, 2)[:, at:at + P], q_buf[:, h * 256 + kb * P:h * 256 + kb * P + P],
                                              ident)
                    mm.then_inc(s_st, 1)

                def swa_out(i):
                    g, t = i // 2, i % 2
                    pe.wait_ge(s_pt, 4 * l + i + 1)
                    if i > 0:
                        pe.wait_ge(s_soe, 4 * l + i)
                    for h in range(4):
                        for kb in range(t + 1):
                            at = (h * (t + 1) + kb) * P
                            val = misc[:, kb * 272 + 144 + g * 64:kb * 272 + 144 + g * 64 + 64]
                            mm = t_.matmul(banks(3)[:, h * 64:h * 64 + 64], k_buf[:, at:at + P], val,
                                           start=kb == 0, stop=kb == t)
                    mm.then_inc(s_so, 1)

                swa_scores(0)
                for i in range(4):
                    merge(i)
                    swa_turn(i)
                    if i < 3:
                        swa_scores(i + 1)
                    swa_out(i)

                def args(i):
                    kind, n, t = ARGS[i]
                    if i > 0:
                        pe.wait_ge(s_exp, NA * l + i)
                    else:
                        pe.wait_ge(s_sst, 4 * l + 4)
                        pe.wait_ge(s_free, gw + 10)
                    if kind == "G":
                        log = log_a[:, t * 256 + n * P:t * 256 + n * P + P]
                    else:
                        log = log_f[:, t * 512 + n * P:t * 512 + n * P + P]
                    col = T_ARG + (1 - t) * P
                    for h in range(2):
                        mm = t_.matmul(ps[:, 4 + h, :], log, tf[:, col + h * N:col + h * N + N], start=True, stop=True)
                    mm.then_inc(s_arg, 1)

                def scores(r):
                    i, j = ROUNDS[r]
                    kind, n, t = ARGS[i]
                    at = rows_of(kind, j)
                    pe.wait_ge(s_qe, NA * l + i + 1)
                    pe.wait_ge(s_ke, NA * l + i + 1)
                    if r > 0:
                        pe.wait_ge(s_mask, NR * l + r)
                    else:
                        pe.wait_ge(s_pt, 4 * l + 4)
                        pe.wait_ge(s_soe, 4 * l + 4)
                    kv = k_buf.rearrange("p (v n) -> p v n", n=P)
                    qv = q_buf.rearrange("p (v n) -> p v n", n=P)
                    for v in range(N_LEVELS):
                        t_.matmul(banks(6, 2)[:, v * P:v * P + P], kv[at, t + v, :], qv[at, t + v, :], start=True, stop=True)
                    mm = t_.matmul(banks(6, 2)[:, 7 * P:8 * P], k_block(kind, n, t)[at, :], q_block(kind, n, t)[at, :],
                                   start=True, stop=True)
                    if t == 1:
                        if cross_before(r) > 0:
                            pe.wait_ge(s_px, NX * l + cross_before(r))
                        mm = t_.matmul(banks(2)[:, 0:P], k_cross[at, :], qv[at, 0, :], start=True, stop=True)
                    mm.then_inc(s_sc, 1)

                def out_of(r):
                    i, j = ROUNDS[r]
                    kind, n, t = ARGS[i]
                    head = 2 * n + j if kind == "G" else n
                    val = v_g if kind == "G" else v_h
                    pe.wait_ge(s_psum, NR * l + r + 1)
                    if r > 0:
                        pe.wait_ge(s_oe, NR * l + r)
                    dst = banks(3)[:, (r % 2) * P:(r % 2) * P + P]
                    mm = t_.matmul(dst, p_sum[:, (r % 2) * P:(r % 2) * P + P], val[:, t * N + head * P:t * N + head * P + P],
                                   start=True, stop=t == 0)
                    if t == 1:
                        pe.wait_ge(s_px, NX * l + cross_before(r) + 1)
                        mm = t_.matmul(dst, p_cross, val[:, head * P:head * P + P], start=False, stop=True)
                    mm.then_inc(s_o, 1)

                args(0)
                for i in range(NA):
                    if i < 8:
                        merge(4 + i)
                    for r in [r for r, (q, _) in enumerate(ROUNDS) if q == i]:
                        if r > 0:
                            out_of(r - 1)
                        scores(r)
                        if ROUNDS[r][1] == 0 and i + 1 < NA:
                            args(i + 1)
                out_of(NR - 1)

                def branch(bi):
                    b = BRANCHES[bi]
                    src = [o_a, o_b, o_c][b]
                    if b != 1:
                        pe.wait_ge(s_heads, 2 * l + (1 if b == 0 else 2))
                    stage_groups(g_layer + 15 + 2 * bi, src)

                def branch_product(bi):
                    pe.wait_ge(s_free, g_layer - 1 + 15 + 2 * bi + 2)
                    for n in range(2):
                        c = 15 + 2 * bi + n
                        if c == 15:
                            pe.wait_ge(s_eva, 30 * l + 30)
                            pe.wait_ge(s_oe, NR * l + NR)
                        elif bi > 0:
                            pe.wait_ge(s_evd, 12 * l + 2 * (2 * (bi - 1) + n + 1))
                        left = lambda k, t: (x_hi[:, (bi % 2) * 1024 + k * SEQ + t * P:(bi % 2) * 1024 + k * SEQ + t * P + P],
                                             x_lo[:, (bi % 2) * 1024 + k * SEQ + t * P:(bi % 2) * 1024 + k * SEQ + t * P + P])
                        product(pe, Unit(base + 30 + 2 * bi + n), left, [ps[:, pair(c) + t, :] for t in range(NT)], N,
                                True, True, 0)

                for bi in range(3):
                    branch(bi)
                    branch_product(bi)
                pe.wait_ge(s_merged, 4 * l + 4)
                for i in range(4):
                    turn_group(g_layer + 21 + i, [merged[:, t * D + k * P:t * D + k * P + P] for k in (2 * i, 2 * i + 1)
                                                  for t in range(NT)])
                pe.wait_ge(s_free, g_layer - 1 + 25)
                for n in range(2):
                    acc = [ps[:, 2 * n + t, :] for t in range(NT)]
                    product(pe, Unit(base + 36 + 2 * n), model_left, acc, N, True, False, 0)
                    product(pe, Unit(base + 37 + 2 * n), model_left, acc, N, False, True, 4)
                norm_groups(2 * l + 1, g_layer + 25)
                pe.wait_ge(s_free, g_layer - 1 + 29)
                if l == 0:
                    ff(U_FFN, 0, 0, FFN_STEPS, NT, model_left, mod_steps=8)
                    pe.wait_ge(s_xupd, 2 * NT)

            pe.wait_ge(s_rsp, 2)
            for t in range(NT):
                for k in range(KD):
                    hi, lo = model_left(k, t)
                    for i, (lhs, rhs) in enumerate(((hi, r_hi), (hi, r_lo), (lo, r_hi), (lo, r_lo))):
                        mm = t_.matmul(banks(6)[:, t * 8:t * 8 + 8], lhs, rhs[:, k * 8:k * 8 + 8],
                                       start=k == 0 and i == 0, stop=k == KD - 1 and i == 3)
            mm.then_inc(s_logit, 1)
            pe.wait_ge(s_m, 1)
            tri, one = tb[:, B_TRI:B_TRI + P], tb[:, B_ONES:B_ONES + P]
            m0, m1 = m_bf[:, 0:8], m_bf[:, 8:16]
            t_.matmul(banks(7)[:, 0:8], tri, m0, start=True, stop=True)
            t_.matmul(banks(7)[:, 8:16], one, m0, start=True, stop=False)
            t_.matmul(banks(7)[:, 8:16], tri, m1, start=False, stop=True)
            t_.matmul(banks(7)[:, 16:24], one, m0, start=True, stop=False)
            t_.matmul(banks(7)[:, 16:24], one, m1, start=False, stop=True).then_inc(s_pos, 1)

            def gather(n):
                pe.wait_ge(s_sel, n)
                for k in range(KD):
                    for t in range(NT):
                        mm = t_.matmul(banks(6, 2)[:, k * P:k * P + P], xhat[:, t * D + k * P:t * D + k * P + P],
                                       sel[:, t * P:t * P + P], start=t == 0, stop=t == NT - 1)
                mm.then_inc(s_gat, 1)

            def item_left(k, t):
                return x_hi[:, k * P:k * P + P], x_lo[:, k * P:k * P + P]

            pe.wait_ge(s_ids, 1)
            items = pe.value_load(ids[0:1, 0:1], min_val=0, max_val=MAX_OVER) + N_EXP
            gather(1)
            with pe.Fori(0, items) as it:
                pe.wait_ge(s_selw, it + 1)
                for t in range(NT):
                    mm = t_.transpose(banks(3)[:, t * P:t * P + P], sel_w[:, t * P:t * P + P], ident)
                mm.then_inc(s_selt, 1)
                pe.wait_ge(s_hglo, it + 1)
                ff(U_MOE, it * MOE_STEPS, it * MOE_STEPS + FFN_STEPS, MOE_STEPS, 1, item_left,
                   last_hook=lambda: gather(it + 2))
                pe.wait_ge(s_ysb, it + 1)
                pe.wait_ge(s_selc, it + 1)
                pe.wait_ge(s_hg, it + 2)
                for t in range(NT):
                    for n in range(2):
                        mm = t_.matmul(ps[:, 6 - 2 * t + n, :], sel_t[:, t * P:t * P + P], y_sb[:, n * N:n * N + N],
                                       start=True, stop=True)
                    mm.then_inc(s_scat, 1)
                pe.wait_ge(s_yadd, 2 * it + 2)


_INS = ['x', 'c', 'w_mod', 'b_mod', 'norm_g', 'w_in', 'gla_w_gate', 'gla_b_gate', 'gla_norm_g', 'swa_sinks', 'hgrn_lb',
        'hgrn_norm_g', 'w_branch', 'w_merge', 'b_merge', 'w_out', 'ffn_w_gate', 'ffn_w_up', 'ffn_w_down', 'moe_router',
        'moe_w_gate', 'moe_w_up', 'moe_w_down']


def shape_tables():
    import numpy as np

    s, t = np.arange(P)[:, None], np.arange(P)[None, :]
    args, masks = [], []
    for v in range(N_LEVELS):
        half = P >> (v + 1)
        mid = t // (2 * half) * (2 * half) + half - 1
        args.append(np.where(t > mid, (s > mid) & (s <= t), (s > t) & (s <= mid)))
        same = s // (2 * half) == t // (2 * half)
        masks.append(same & (t > mid) & (s <= mid))
    prefix, suffix = s <= t, s > t
    f32 = np.concatenate([np.eye(P, dtype=bool), prefix] + args + [suffix], axis=1).astype(np.float32)
    chunk = 64

    def dist(q0, n):
        q, k = q0 + np.arange(P)[:, None], np.arange(n)[None, :]
        seen = (k // chunk <= q // chunk) & (k // chunk >= q // chunk - 1)
        return np.where(seen, np.abs(q - k), NEVER)

    zero = np.zeros((P, P))
    bf = np.concatenate([np.concatenate(masks + [s == t], axis=1).astype(np.float64), dist(0, P), dist(P, 2 * P),
                         (s < t).astype(np.float64), np.broadcast_to(t, (P, P)).astype(np.float64), zero + 1, zero], axis=1)
    return {"table_f32": f32, "table_bf16": bf.astype(mybir.dt.np(BF16)), "ones_row": np.ones((1, SEQ), np.float32)}


def kernel(**inputs):
    import numpy as _np
    import concourse.bacc as _bacc
    from concourse import mybir as _mybir
    from concourse.bass_utils import run_bass_kernel_spmd as _run

    nc = _bacc.Bacc("TRN2", target_bir_lowering=False, num_devices=1)
    arrays, args = {}, {}
    given = {name: _np.ascontiguousarray(inputs[name]) for name in _INS}
    given.update(shape_tables())
    for name, arr in given.items():
        arrays[f"in_{name}_dram"] = arr
        args[name] = nc.dram_tensor(f"in_{name}_dram", arr.shape, _mybir.dt.from_np(arr.dtype),
                                    kind="ExternalInput").ap()
    out = nc.dram_tensor("out_0_dram", (1, SEQ, D), _mybir.dt.float32, kind="ExternalOutput").ap()
    program(nc, args, out)
    r = _run(nc, [arrays], core_ids=[0])
    return r.results[0]["out_0_dram"]
```

```python
from contextlib import ExitStack

import concourse.bass as bass
from concourse import mybir

F32 = mybir.dt.float32
F32R = mybir.dt.float32r
BF16 = mybir.dt.bfloat16
I32 = mybir.dt.int32
ALU = mybir.AluOpType
ACT = mybir.ActivationFunctionType
AX = mybir.AxisListType

P = 128
D = 1024
KD = D // P
SEQ = 256
NT = SEQ // P
DEPTH = 2
EPS = 1e-6
D_IN = 4368
D_FF = 2816
D_FFE = 3584
N_EXP = 8
ITEMS = 12
MAX_OVER = 3
FF = 256
N = 512
RING = 3

GQ, GK, GV, GG, GLR, SQ, SK, SV, HQ, HF, HI, HG = 0, 256, 512, 1024, 1536, 1552, 2064, 2192, 2320, 2832, 3344, 3856
W_IN_CHUNKS = [(HF, 512), (HQ, 512), (GQ, 512), (None, 272), (SQ, 512), (GV, 512), (HI, 512), (GG, 512), (HG, 512)]
N_WIN = len(W_IN_CHUNKS)
N_MERGE = 6
MIX_UNITS = 2 * (N_WIN + N_MERGE + 2) + 6
FFN_STEPS = D_FF // FF
MOE_STEPS = D_FFE // FF
U_FFN = MIX_UNITS
U_MIX1 = MIX_UNITS + 3 * FFN_STEPS
U_MOE = U_MIX1 + MIX_UNITS

R_BMOD, R_NORM, R_MERGE, N_ROWS = 0, 24, 40, 52

T_ID, T_ARG = 0, 128
T_F32 = 128 + 9 * 128
B_MASK, B_DIST, B_TRI, B_IOTA, B_ONES, B_ZERO = 0, 1024, 1408, 1536, 1664, 1792
T_BF16 = 1920
N_LEVELS = 7
POOL_LEVELS = 4
FIRST_MOD = 4
MOD_UNITS = 2 * FIRST_MOD
NEVER = 1e33


class Chain:

    def __init__(self, eng, sem, base=0):
        self.eng, self.sem, self.n, self.base = eng, sem, 0, base

    def link(self, ins):
        self.n += 1
        ins.then_inc(self.sem, 1)
        self.eng.wait_ge(self.sem, self.base + self.n)


class Unit:

    def __init__(self, s, d=0):
        self.s, self.d, self.slot = s, d, (s + MOD_UNITS) % RING
        self.number = 3 * d + s
        self.landed = 32 * (d + (s + MOD_UNITS) // RING + 1)


def program(nc, a, out):
    with ExitStack() as ctx:
        def sb(name, shape, dt=F32):
            return ctx.enter_context(nc.sbuf_tensor(name, shape, dt))

        def sem(name):
            return ctx.enter_context(nc.semaphore(name))

        ring = sb("ring", [P, RING, 2048])
        w_hi = sb("w_hi", [P, RING, 2048], F32R)
        w_lo = sb("w_lo", [P, RING, 2048], F32R)
        x_hi = sb("x_hi", [P, KD * SEQ], F32R)
        x_lo = sb("x_lo", [P, KD * SEQ], F32R)
        a_hi = sb("a_hi", [P, 2 * SEQ], F32R)
        a_lo = sb("a_lo", [P, 2 * SEQ], F32R)
        r_hi = sb("r_hi", [P, KD * N_EXP], F32R)
        r_lo = sb("r_lo", [P, KD * N_EXP], F32R)
        tf = sb("tf", [P, T_F32])
        tb = sb("tb", [P, T_BF16], BF16)
        rows = sb("rows", [N_ROWS, N])
        row_cols = sb("row_cols", [P, 4, N_ROWS])
        ones = sb("ones", [P, 1])
        warm = sb("warm", [P, 1])
        gate_w = sb("gate_w", [17, DEPTH, 256])
        glr_t = sb("glr_t", [17, SEQ])
        head_gain = sb("head_gain", [P, 2 * P])
        sinks = sb("sinks", [P, DEPTH * 8])
        c_rows = sb("c_rows", [KD, P])
        c_col = sb("c_col", [P, KD])
        mod_col = sb("mod_col", [P, DEPTH * 12, 4])
        s_col = sb("s_col", [P, KD])
        b_col = sb("b_col", [P, KD])
        col_tmp = sb("col_tmp", [P, 4])
        ssq = sb("ssq", [P, 16])
        var = sb("var", [P, 8])
        sd = sb("sd", [P, 8])
        rs = sb("rs", [P, 8])
        soft = sb("soft", [P, 8, 4])
        rden = sb("rden", [P, 2, 4])
        mem_words = 2048 + 2048 + 1024 * 2 + 544 + 256 + 4608 + 1536 + 4096 + 1024 + 4096 + 512
        mem = sb("mem", [P, mem_words])
        ids = sb("ids", [1, 4], I32)
        m_bf = sb("m_bf", [P, NT * N_EXP], BF16)
        at = [0]

        def carve(words):
            at[0] += words
            return mem[:, at[0] - words:at[0]]

        x = carve(2048)
        v_h, gate_h = x[:, 0:1024], x[:, 1024:2048]
        g_rows = carve(2048)
        v_g, gate_g = carve(1024), carve(1024)
        misc, sk_swap = carve(544), carve(256)
        ft = carve(4608)
        log_a, log_f = carve(512), carve(1024)
        gates = carve(4096)
        o_b = carve(1024)
        work = carve(4096)
        p_sum, p_cross, k_cross = carve(256), carve(128), carve(128)

        o_a, o_c, merged = ft[:, 0:1024], ft[:, 1536:2560], ft[:, 2560:4608]
        stage_f, stage_k, stage_q, stage_g = [gates[:, 1024 * i:1024 * i + 1024] for i in range(4)]
        xhat = gates[:, 0:2048]
        e_buf, q_buf, k_buf, p_buf = [work[:, 1024 * i:1024 * i + 1024] for i in range(4)]
        mod_ring = work[:, 0:2048].rearrange("p (s n) -> p s n", n=N)
        mod_acc = work[:, 2048:3072].rearrange("p (s n) -> p s n", n=N)
        lb_row, om_row = work[:, 3072:3584], work[:, 3584:4096]
        h_tmp = mem[:, at[0] - 512 - 4096 - 1024 - 4096 - 1536:][:, 0:1024].rearrange("p (b n) -> p b n", n=512)
        silu_buf, act_buf = v_g[:, 0:512], v_g[:, 512:1024]
        y_acc, y_sb, hg_tmp = ft[:, 0:2048], ft[:, 2048:3072], ft[:, 3072:4096]
        sel, sel_w, sel_t = gate_g[:, 0:256], gate_g[:, 256:512], gate_g[:, 512:768]
        cur = gate_g[:, 768:776]
        pos_items = gate_g[:, 776:776 + 2 * ITEMS].rearrange("p (i t) -> p i t", t=NT)
        w_items = gate_g[:, 800:800 + 2 * ITEMS].rearrange("p (i t) -> p i t", t=NT)
        r_raw = misc[:, 0:64]
        logit_rows = work[0:N_EXP, 1152:1152 + SEQ]
        rt = work[:, 0:1024].rearrange("p (i n) -> p i n", n=16)

        ident = tf[:, T_ID:T_ID + P]
        ps = ctx.enter_context(nc.psum_tensor("ps", [P, 8, N], F32))

        def banks(i, k=1):
            return ps[:, i:i + k, :].rearrange("p b n -> p (b n)")

        s_const = sem("constants_landed")
        s_rows = sem("rows_landed")
        s_c = sem("c_landed")
        s_par = sem("head_parameters_landed")
        s_lb = sem("lower_bounds_landed")
        s_xin = sem("x_landed")
        s_xre = sem("x_back")
        s_gain = sem("head_gains_landed")
        s_park = sem("x_parked")
        s_router = sem("router_landed")
        s_unit = [sem(f"unit_landed{i}") for i in range(RING)]
        s_hi = sem("unit_hi")
        s_lo = sem("unit_lo")
        s_used = sem("unit_used")
        s_mod = [sem(f"mod_landed{i}") for i in range(2)]
        s_macc = sem("mod_accumulated")
        s_mps = sem("mod_summed")
        s_mev = sem("mod_taken")
        s_dch = sem("vector_chain")
        s_ach = sem("scalar_chain")
        s_sq = sem("squares_summed")
        s_var = sem("variance_ready")
        s_sd = sem("deviation_ready")
        s_xhat = sem("xhat_ready")
        s_xupd = sem("x_updated")
        s_tr = sem("group_turned")
        s_tmp = sem("group_scaled")
        s_ghi = sem("group_hi")
        s_free = sem("group_taken")
        s_eva = sem("chunk_taken_scalar")
        s_evd = sem("chunk_taken_vector")
        s_kc = sem("sigmoid_ready")
        s_kr = sem("stage_k_ready")
        s_lbd = sem("bounds_shifted")
        s_lbe = sem("bounds_exp")
        s_f1 = sem("f_negated")
        s_f2 = sem("f_exponent")
        s_f3 = sem("f_bounded")
        s_f4 = sem("f_log_parts")
        s_logf = sem("log_f_ready")
        s_swap = sem("sk_swapped")
        s_la = sem("log_a_part")
        s_cs = sem("c_silu")
        s_ss = sem("swa_scores")
        s_sst = sem("swa_scores_taken")
        s_nm = sem("swa_max_ready")
        s_pr = sem("swa_probs")
        s_st = sem("swa_probs_turned")
        s_pt = sem("swa_turned_copied")
        s_so = sem("swa_out")
        s_soe = sem("swa_out_taken")
        s_arg = sem("decay_args")
        s_exp = sem("decay_exp")
        s_qe = sem("q_decayed")
        s_ke = sem("k_decayed")
        s_sc = sem("scan_scores")
        s_mask = sem("scan_masked")
        s_psum = sem("scan_summed")
        s_px = sem("scan_cross")
        s_o = sem("scan_out")
        s_oe = sem("scan_out_taken")
        s_heads = sem("heads_normed")
        s_merged = sem("merged_ready")
        s_fsilu = sem("ff_silu")
        s_fact = sem("ff_act")
        s_ftr = sem("ff_act_turned")
        s_fhi = sem("ff_act_hi")
        s_flo = sem("ff_act_lo")
        s_logit = sem("logits_ready")
        s_lrow = sem("logit_rows_copied")
        s_m = sem("choice_ready")
        s_pos = sem("positions_ready")
        s_top = sem("top_difference")
        s_tope = sem("top_exponent")
        s_rsp = sem("router_split")
        s_ids = sem("item_tables_ready")
        s_selw = sem("sel_w_ready")
        s_sel = sem("sel_ready")
        s_selt = sem("sel_turned")
        s_selc = sem("sel_t_ready")
        s_gat = sem("gathered")
        s_hg = sem("gathered_scaled")
        s_hghi = sem("gathered_hi")
        s_hglo = sem("gathered_lo")
        s_yzero = sem("y_zeroed")
        s_ysb = sem("y_copied")
        s_scat = sem("scattered")
        s_yadd = sem("y_added")
        s_mdch = sem("moe_vector_chain")
        s_out = sem("out_written")

        def w_src(ap, col, width, k0, blocks=4):
            return ap.rearrange("(k p) n -> p k n", p=P)[:, k0:k0 + blocks, col:col + width]

        def load(sp, u, parts):
            if u.d is not 0 or u.s >= RING:
                sp.wait_ge(s_lo, u.number - (RING - 1))
            elif u.s + MOD_UNITS >= RING:
                sp.wait_ge(s_macc, 4 * (u.s + MOD_UNITS - (RING - 1)))
            for dst, src in parts:
                sp.dma_start(dst, src).then_inc(s_unit[u.slot], 16)

        def load_plain(sp, u, ap, col, width, k0):
            dst = ring[:, u.slot, :].rearrange("p (k n) -> p k n", n=N)
            src = w_src(ap, col, width, k0)
            load(sp, u, [(dst[:, 0:2, 0:width], src[:, 0:2, :]), (dst[:, 2:4, 0:width], src[:, 2:4, :])])

        def load_misc(sp, u, ap, k0):
            dst = ring[:, u.slot, :].rearrange("p (k n) -> p k n", n=N)
            load(sp, u, [(dst[:, :, 0:16], w_src(ap, GLR, 16, k0)), (dst[:, :, 16:272], w_src(ap, SK, 256, k0))])

        def load_up(sp, u, gate, up, e, j, k0):
            dst = ring[:, u.slot, :].rearrange("p (k n) -> p k n", n=N)
            parts = []
            for half, w in ((0, gate), (1, up)):
                src = w.rearrange("e (k p) f -> e p k f", p=P)[bass.ds(e, 1), :, k0:k0 + 4, bass.ds(j * FF, FF)]
                parts.append((dst[:, :, half * FF:half * FF + FF], src.rearrange("o p k f -> (o p) k f")))
            load(sp, u, parts)

        def load_down(sp, u, down, e, j):
            dst = ring[:, u.slot, :].rearrange("p (k n) -> p k n", n=D)
            view = down.rearrange("e (r p) n -> e p r n", p=P)
            parts = []
            for k in range(2):
                src = view[bass.ds(e, 1), :, bass.ds(j * 2 + k, 1), :]
                parts.append((dst[:, k, :], src.rearrange("o p k n -> (o p) (k n)")))
            load(sp, u, parts)

        def unit_view(buf, u, width):
            v = buf[:, u.slot, :]
            return v if width is None else v.rearrange("p (k n) -> p k n", n=N)[:, :, 0:width]

        def split_hi(act, u, width=None):
            act.wait_ge(s_unit[u.slot], u.landed)
            if u.d is not 0 or u.s >= RING:
                act.wait_ge(s_used, u.number - (RING - 1))
            nc.scalar.activation(unit_view(w_hi, u, width), unit_view(ring, u, width), ACT.Copy).then_inc(s_hi, 1)

        def split_lo(dve, u, width=None):
            dve.wait_ge(s_hi, u.number + 1)
            nc.vector.tensor_tensor(unit_view(w_lo, u, width), unit_view(ring, u, width),
                                    unit_view(w_hi, u, width).bitcast(F32), ALU.subtract).then_inc(s_lo, 1)

        def narrow(n):
            m = n if n < MIX_UNITS else n - U_MIX1
            return 272 if 0 <= m < 2 * N_WIN and W_IN_CHUNKS[m // 2][0] is None else None

        class Splits:

            def __init__(self, eng, split):
                self.eng, self.split, self.n = eng, split, 0

            def upto(self, n, end):
                while self.n < min(n, end):
                    self.split(self.eng, Unit(self.n), narrow(self.n))
                    self.n += 1

        def product(pe, u, left, acc, width, first, last, k0=0, groups=NT):
            wh = w_hi[:, u.slot, :].rearrange("p (k n) -> p k n", n=N)
            wl = w_lo[:, u.slot, :].rearrange("p (k n) -> p k n", n=N)
            pe.wait_ge(s_lo, u.number + 1)
            for k in range(4):
                for t in range(groups):
                    hi, lo = left(k0 + k, t)
                    for i, (l, r) in enumerate(((hi, wh), (hi, wl), (lo, wh))):
                        mm = nc.tensor.matmul(acc[t], l, r[:, k, 0:width], start=first and k == 0 and i == 0,
                                              stop=last and k == 3 and i == 2, skip_group_check=True)
            mm.then_inc(s_used, 1)

        def model_left(k, t):
            at = k * SEQ + t * P
            return x_hi[:, at:at + P], x_lo[:, at:at + P]

        G_LAYER = 4 + 11 + 6 + 4 + 4

        def group_bank(g):
            return banks(4 + g % 2)

        def swa_bank(h):
            return ps[:, 4 + h % 2, (h // 2) * 256:(h // 2) * 256 + 256]

        MOD_COLS1 = [0, 1, 2, 3, 6, 7, 8, 9]
        MOD = [(0, c) for c in range(12)] + [(1, c) for c in MOD_COLS1] + [(1, c) for c in (4, 5, 10, 11)]

        def mod_of_win(l, c):
            if l == 0:
                return 4 + c if c < 8 else None
            return 20 + c if c < 4 else None

        ARGS = [("G", p, t) for p in range(2) for t in range(NT)] + [("H", h, t) for h in range(4) for t in range(NT)]
        ROUNDS = [(i, j) for i, (kind, _, _) in enumerate(ARGS) for j in range(2 if kind == "G" else 1)]
        NA, NR = len(ARGS), len(ROUNDS)
        CROSS = [r for r, (i, _) in enumerate(ROUNDS) if ARGS[i][2] == 1]
        NX = len(CROSS)
        HEADS_STEP = 6

        def rounds_before(i):
            return sum(1 for q, _ in ROUNDS if q < i)

        def cross_before(r):
            return sum(1 for q in CROSS if q < r)

        def rows_of(kind, j):
            return slice(64 * j, 64 * j + 64) if kind == "G" else slice(0, P)

        def ft_block(b, t=None):
            return ft[:, b * SEQ:b * SEQ + SEQ] if t is None else ft[:, b * SEQ + t * P:b * SEQ + t * P + P]

        def q_block(kind, i, t):
            return ft_block((6 if kind == "G" else 10) + i, t)

        def k_block(kind, i, t):
            return ft_block((8 if kind == "G" else 14) + i, t)

        def merge_gate(m, t):
            buf = gates[:, m * 1024:m * 1024 + 1024] if m < 4 else (v_g if m == 4 else e_buf)
            return buf[:, t * N:t * N + N]

        def pair(c):
            if c < N_WIN:
                return 2 * (c % 2)
            return 0 if c < 15 else 2 * ((c - 15) % 2)

        BRANCHES = [1, 0, 2]

        block = ctx.enter_context(nc.Block())

        @block.sync
        def _(sp):
            def mix_units(l, base):
                u = base
                for col, width in W_IN_CHUNKS:
                    for k0 in (0, 4):
                        if col is None:
                            load_misc(sp, Unit(u), a["w_in"][l], k0)
                        else:
                            load_plain(sp, Unit(u), a["w_in"][l], col, width, k0)
                        u += 1
                for m in range(N_MERGE):
                    for k0 in (0, 4):
                        load_plain(sp, Unit(u), a["w_merge"][l], m * N, N, k0)
                        u += 1
                for b in BRANCHES:
                    for n in range(2):
                        load_plain(sp, Unit(u), a["w_branch"][l, b], n * N, N, 0)
                        u += 1
                for n in range(2):
                    for k0 in (0, 4):
                        load_plain(sp, Unit(u), a["w_out"][l], n * N, N, k0)
                        u += 1

            def ff_units(base, d0, gate, up, down, e, steps):
                load_up(sp, Unit(base, d0), gate, up, e, 0, 0)
                load_up(sp, Unit(base + 1, d0), gate, up, e, 0, 4)
                with sp.Fori(0, steps - 1) as i:
                    load_up(sp, Unit(base + 2, d0 + i), gate, up, e, i + 1, 0)
                    load_up(sp, Unit(base + 3, d0 + i), gate, up, e, i + 1, 4)
                    load_down(sp, Unit(base + 4, d0 + i), down, e, i)
                load_down(sp, Unit(base + 2, d0 + (steps - 1)), down, e, steps - 1)

            def mod_unit(m):
                load_plain(sp, Unit(m - MOD_UNITS), a["w_mod"][0], MOD[m // 2][1] * N, N, 4 * (m % 2))

            sp.dma_start(c_rows[:], a["c"].rearrange("b (k p) -> (b k) p", p=P)).then_inc(s_c, 16)
            sp.dma_start(tf[:], a["table_f32"]).then_inc(s_const, 16)
            sp.dma_start(rows[0:24, :], a["b_mod"].rearrange("l (c n) -> (l c) n", n=N)).then_inc(s_rows, 16)
            sp.dma_start(rows[24:40, :], a["norm_g"].rearrange("l i (h n) -> (l i h) n", n=N)).then_inc(s_rows, 16)
            sp.dma_start(rows[40:52, :], a["b_merge"].rearrange("l (m n) -> (l m) n", n=N)).then_inc(s_rows, 16)
            for u in range(RING):
                mod_unit(u)
            sp.dma_start(x.rearrange("p (t d) -> p t d", d=D), a["x"].rearrange("b (t p) d -> (b p) t d", p=P)) \
                .then_inc(s_xin, 16)
            sp.dma_start(tb[:], a["table_bf16"]).then_inc(s_par, 16)
            sp.dma_start(gate_w[0:16, :, :], a["gla_w_gate"].rearrange("l r n -> r l n")).then_inc(s_par, 16)
            sp.dma_start(gate_w[16:17, :, :], a["gla_b_gate"].rearrange("l n -> (l n)").unsqueeze(0)
                         .rearrange("o (l n) -> o l n", n=256)).then_inc(s_par, 16)
            sp.dma_start(glr_t[16:17, :], a["ones_row"]).then_inc(s_par, 16)
            sp.dma_start(sinks[:], a["swa_sinks"].rearrange("l h -> (l h)").unsqueeze(0).to_broadcast([P, 16])) \
                .then_inc(s_par, 16)
            for u in range(RING, MOD_UNITS):
                mod_unit(u)
            mix_units(0, 0)
            ff_units(U_FFN, 0, a["ffn_w_gate"], a["ffn_w_up"], a["ffn_w_down"], 0, FFN_STEPS)
            mix_units(1, U_MIX1)
            wg, wu, wd = [a[n].rearrange("o e k n -> (o e) k n") for n in ("moe_w_gate", "moe_w_up", "moe_w_down")]
            with sp.Fori(0, N_EXP) as e:
                ff_units(U_MOE, e * MOE_STEPS, wg, wu, wd, e, MOE_STEPS)
            sp.wait_ge(s_ids, 1)
            over = sp.value_load(ids[0:1, 0:1], min_val=0, max_val=MAX_OVER)
            with sp.If(over > 0):
                with sp.Fori(0, over) as r:
                    e = sp.value_load(ids[0:1, bass.ds(r + 1, 1)], min_val=0, max_val=N_EXP - 1)
                    ff_units(U_MOE, (r + N_EXP) * MOE_STEPS, wg, wu, wd, e, MOE_STEPS)
            sp.wait_ge(s_xupd, 2 * 2 * NT)
            sp.dma_start(out.rearrange("b (t p) d -> (b p) t d", p=P), x.rearrange("p (t d) -> p t d", d=D)) \
                .then_inc(s_out, 16)
            sp.wait_ge(s_out, 16)
            sp.wait_ge(s_park, 16)

        @block.gpsimd
        def _(pool):
            def mod_load(q, l, col, first=False):
                for k in range(0, KD, 2):
                    s = k % 4
                    if not (first and k < 4):
                        pool.wait_ge(s_macc, 8 * q + (k - 2))
                    src = w_src(a["w_mod"][l], 0, 6 * D, k, 2)[:, :, bass.ds(col, N)]
                    pool.dma_start(mod_ring[:, s:s + 2, :], src).then_inc(s_mod[s // 2], 16)

            nc.gpsimd.memset(ones[:], 1.0).then_inc(s_const, 1)
            for l in range(DEPTH):
                if l == 1:
                    pool.wait_ge(s_heads, 2)
                for i, name in enumerate(("gla_norm_g", "hgrn_norm_g")):
                    pool.dma_start(head_gain[:, i * P:i * P + P], a[name][l:l + 1, :].to_broadcast([P, P])) \
                        .then_inc(s_gain, 16)
                if l == 1:
                    pool.wait_ge(s_sd, 6 + 1)
                    pool.dma_start(o_b, a["hgrn_lb"].rearrange("l n -> (l n)").unsqueeze(0).to_broadcast([P, 1024])) \
                        .then_inc(s_lb, 16)
                for c in range(N_WIN):
                    q = mod_of_win(l, c)
                    if q is not None:
                        mod_load(q, l, MOD[q][1] * N, first=q == FIRST_MOD)
                for i, (kind, n, t) in enumerate(ARGS):
                    pool.wait_ge(s_exp, l * NA + i + 1)
                    if i == 0:
                        pool.wait_ge(s_free, l * G_LAYER + 16)
                        pool.wait_ge(s_so, 4 * l + 4)
                    else:
                        pool.wait_ge(s_sc, l * NR + rounds_before(i))
                    ev = e_buf.rearrange("p (v n) -> p v n", n=P)
                    kv = k_buf.rearrange("p (v n) -> p v n", n=P)
                    key = k_block(kind, n, t)
                    if t == 0:
                        nc.gpsimd.tensor_tensor(k_cross, ev[:, 7, :], key, ALU.mult)
                    nc.gpsimd.tensor_tensor(kv[:, t:t + POOL_LEVELS, :], ev[:, t:t + POOL_LEVELS, :],
                                            key[:, None, :].to_broadcast([P, POOL_LEVELS, P]), ALU.mult) \
                        .then_inc(s_ke, 1)
                pool.wait_ge(s_heads, 2 * l + 2)
                if l == 1:
                    pool.wait_ge(s_park, 16)
                src = a["x"] if l == 0 else out
                pool.dma_start(x.rearrange("p (t d) -> p t d", d=D), src.rearrange("b (t p) d -> (b p) t d", p=P)) \
                    .then_inc(s_xre, 16)
                if l == 0:
                    pool.wait_ge(s_evd, 12)
                    with pool.Fori(0, 8) as i:
                        mod_load(i + 12, 1, i * N + (i // 4) * (2 * N))
                    pool.wait_ge(s_xupd, 2 * NT)
                    pool.dma_start(out.rearrange("b (t p) d -> (b p) t d", p=P), x.rearrange("p (t d) -> p t d", d=D)) \
                        .then_inc(s_park, 16)
                if l == 1:
                    pool.wait_ge(s_evd, 24)
                    pool.dma_start(r_raw.rearrange("p (k e) -> p k e", e=N_EXP),
                                   a["moe_router"].rearrange("o (k p) e -> (o p) k e", p=P)).then_inc(s_router, 16)

        @block.scalar
        def _(act):
            ch = Chain(act, s_ach)
            sp_ = Splits(act, split_hi)

            def deviation(n, width=2):
                act.wait_ge(s_var, n + 1)
                nc.scalar.activation(sd[:, 0:width], var[:, 0:width], ACT.Sqrt).then_inc(s_sd, 1)

            def group_hi(src, dst):
                nc.scalar.activation(dst, src, ACT.Copy).then_inc(s_ghi, 1)

            squares = [0]

            def square(src, t, dst=None):
                if squares[0]:
                    act.wait_ge(s_sq, squares[0])
                nc.scalar.activation(o_b if dst is None else dst, src, ACT.Square, accum_out=ssq[:, t:t + 1]) \
                    .then_inc(s_sq, 1)
                squares[0] += 1

            def norm(n, r):
                for t in range(NT):
                    if n > 0:
                        act.wait_ge(s_xupd, NT * (n - 1) + t + 1)
                    square(x[:, t * D:t * D + D], t, xhat[:, t * D:t * D + D])
                deviation(r)
                for i in range(4):
                    act.wait_ge(s_tmp, 4 * n + i + 1)
                    group_hi(h_tmp[:, i % 2, :], x_hi[:, i * 512:i * 512 + 512])

            def copy(dst, src, scale=1.0, fn=ACT.Copy):
                return nc.scalar.activation(dst, src, fn, scale=scale)

            def ff(base, d0, f0, steps, nt, first=None, early=(), behind=None):
                def silu(j, used):
                    act.wait_ge(s_used, used)
                    act.wait_ge(s_fact, f0 + j)
                    nc.scalar.activation(silu_buf.rearrange("p (t n) -> p t n", n=FF)[:, 0:nt, :], ps[:, 0:nt, 0:FF],
                                         ACT.Silu).then_inc(s_fsilu, 1)

                def act_hi(j):
                    act.wait_ge(s_ftr, f0 + j + 1)
                    w = 2 * nt * P
                    nc.scalar.activation(a_hi[:, 0:w], banks(2)[:, 0:w], ACT.Copy).then_inc(s_fhi, 1)

                def step(j, used):
                    split_hi(act, Unit(base + 2, d0 + j))
                    silu(j, used)
                    split_hi(act, Unit(base + 3, d0 + j))
                    act_hi(j)
                    split_hi(act, Unit(base + 4, d0 + j))

                split_hi(act, Unit(base, d0))
                split_hi(act, Unit(base + 1, d0))
                if first:
                    first()
                for j, extra in enumerate(early or (None,)):
                    step(j, Unit(base + 2, d0).number if j == 0 else Unit(base + 1, d0 + j).number)
                    if extra:
                        extra()
                with act.Fori(len(early) or 1, steps - 1) as j:
                    step(j, Unit(base + 1, d0 + j).number)
                last = steps - 1
                split_hi(act, Unit(base + 2, d0 + last))
                silu(last, Unit(base + 1, d0 + last).number)
                if behind:
                    behind()
                act_hi(last)

            act.wait_ge(s_tr, 1)
            nc.scalar.activation(c_col[:], banks(4)[:, 0:KD], ACT.Silu).then_inc(s_cs, 1)
            for l in range(DEPTH):
                base = l * U_MIX1
                end = base + MIX_UNITS
                g_layer = 2 + l * G_LAYER
                sp_.n = base

                if l == 0:
                    act.wait_ge(s_xin, 16)
                sp_.upto(base + 2, end)
                norm(2 * l, 6 * l)
                if l == 1:
                    act.wait_ge(s_lbd, 1)
                    nc.scalar.activation(o_b, o_b, ACT.Exp).then_inc(s_lbe, 1)
                    act.wait_ge(s_park, 16)

                def evac_win(c):
                    act.wait_ge(s_used, base + 2 * c + 2)
                    if c == 1:
                        act.wait_ge(s_tr, g_layer + 4)
                    for t in range(NT):
                        src = ps[:, pair(c) + t, :]
                        w = slice(t * N, t * N + N)
                        if c == 0:
                            ins = copy(stage_f[:, w], src)
                        elif c == 1:
                            ins = copy(stage_q[:, w], src, fn=ACT.Silu)
                        elif c == 2:
                            copy(stage_g[:, t * N:t * N + 256], src[:, 0:256], scale=0.125)
                            ins = copy(stage_g[:, t * N + 256:t * N + 512], src[:, 256:512])
                        elif c == 3:
                            ins = copy(misc[:, t * 272:t * 272 + 272], src[:, 0:272])
                        elif c == 4:
                            if t == 0:
                                act.wait_ge(s_logf, l + 1)
                            ins = copy(stage_f[:, w], src, scale=0.125)
                        elif c == 5:
                            ins = copy(v_g[:, w], src)
                        elif c == 6:
                            ins = copy(v_h[:, w], src)
                        elif c == 7:
                            ins = copy(gate_g[:, w], src, fn=ACT.Silu)
                        else:
                            ins = copy(gate_h[:, w], src, fn=ACT.Silu)
                        ins.then_inc(s_eva, 1)

                for c in range(N_WIN + 1):
                    if c > 0:
                        evac_win(c - 1)
                    if c == 1:
                        act.wait_ge(s_xhat, (2 * l + 1) * NT)
                        act.wait_ge(s_eva, 30 * l + 2)
                        nc.scalar.activation(stage_k, stage_f, ACT.Sigmoid, scale=-1.0).then_inc(s_kc, 1)
                        ch.link(nc.scalar.activation(gate_h, stage_f, ACT.Abs))
                        ch.link(nc.scalar.activation(gate_h, gate_h, ACT.Exp, scale=-1.0))
                        nc.scalar.activation(gate_h, gate_h, ACT.Ln, bias=1.0).then_inc(s_f4, 1)
                    if c == 2:
                        act.wait_ge(s_f1, l + 1)
                        nc.scalar.activation(gate_g, gate_g, ACT.Exp).then_inc(s_f2, 1)
                    if c == 3:
                        act.wait_ge(s_f3, l + 1)
                        nc.scalar.activation(gate_g, gate_g, ACT.Ln, bias=1.0).then_inc(s_f4, 1)
                    if c == 4:
                        act.wait_ge(s_eva, 30 * l + 8)
                        for t in range(NT):
                            m = t * 272
                            copy(sk_swap[:, t * P:t * P + 64], misc[:, m + 80:m + 144]).then_inc(s_swap, 1)
                            copy(sk_swap[:, t * P + 64:t * P + P], misc[:, m + 16:m + 80]).then_inc(s_swap, 1)
                    if c == 6:
                        g = g_layer + 4 + 10
                        act.wait_ge(s_tr, g + 1)
                        z = stage_q[:, 0:512]
                        ch.link(nc.scalar.activation(z, group_bank(g), ACT.Abs))
                        ch.link(nc.scalar.activation(z, z, ACT.Exp, scale=-1.0))
                        nc.scalar.activation(z, z, ACT.Ln, bias=1.0).then_inc(s_la, 1)
                    sp_.upto(min(base + 2 * c + 4, base + 2 * N_WIN + 3), end)

                def swa_exp(i):
                    w = P * (i % 2 + 1)
                    act.wait_ge(s_nm, 4 * l + i + 1)
                    for h in range(4):
                        nc.scalar.activation(q_buf[:, h * 256:h * 256 + w], e_buf[:, h * 256:h * 256 + w], ACT.Exp,
                                             bias=soft[:, 1, h:h + 1], accum_out=soft[:, 3, h:h + 1])
                    nc.scalar.activation(soft[:, 4, :], soft[:, 2, :], ACT.Exp).then_inc(s_pr, 1)

                def merge_done(k):
                    if k % 2 == 0:
                        return
                    m = k // 2
                    act.wait_ge(s_used, base + 2 * (N_WIN + m) + 2)
                    if m == 0:
                        act.wait_ge(s_free, g_layer + 14)
                    if m == 4:
                        act.wait_ge(s_o, NR * l + 8)
                    if m == 5:
                        act.wait_ge(s_qe, NA * l + NA)
                        act.wait_ge(s_ke, NA * l + NA)
                    for t in range(NT):
                        nc.scalar.activation(merge_gate(m, t), ps[:, t, :], ACT.Sigmoid).then_inc(s_eva, 1)

                swa_exp(0)
                for i in range(4):
                    act.wait_ge(s_st, 4 * l + i + 1)
                    if i > 0:
                        act.wait_ge(s_so, 4 * l + i)
                    nb = 4 * (i % 2 + 1)
                    nc.scalar.activation(k_buf[:, 0:nb * P], banks(6, 2)[:, 0:nb * P], ACT.Copy).then_inc(s_pt, 1)
                    merge_done(i)
                    sp_.upto(base + 2 * N_WIN + i + 3, end)
                    if i < 3:
                        swa_exp(i + 1)

                def decay(i):
                    act.wait_ge(s_arg, NA * l + i + 1)
                    if i > 0:
                        act.wait_ge(s_qe, NA * l + i)
                        act.wait_ge(s_ke, NA * l + i)
                    nc.scalar.activation(e_buf, banks(4, 2), ACT.Exp).then_inc(s_exp, 1)

                def out_taken(r):
                    i, j = ROUNDS[r]
                    kind, n, t = ARGS[i]
                    act.wait_ge(s_o, NR * l + r + 1)
                    head = 2 * n + j if kind == "G" else n
                    dst = (o_a if kind == "G" else o_c)[:, t * N + head * P:t * N + head * P + P]
                    nc.scalar.activation(dst, banks(3)[:, (r % 2) * P:(r % 2) * P + P], ACT.Copy).then_inc(s_oe, 1)

                decay(0)
                for i in range(NA):
                    for r in [r for r, (q, _) in enumerate(ROUNDS) if q == i]:
                        if ROUNDS[r][1] == 0 and i + 1 < NA:
                            decay(i + 1)
                        if r > 0:
                            out_taken(r - 1)
                        if ARGS[i][2] == 1:
                            act.wait_ge(s_sc, NR * l + r + 1)
                            nc.scalar.activation(p_cross, banks(2)[:, 0:P], ACT.Copy).then_inc(s_px, 1)
                    if i == HEADS_STEP:
                        deviation(6 * l + 1, 8)
                    if i < 7:
                        merge_done(4 + i)
                        sp_.upto(base + 2 * N_WIN + 4 + i + 3, end)
                out_taken(NR - 1)
                merge_done(11)

                def branch_hi(bi):
                    g = g_layer + 15 + 2 * bi
                    for i in range(2):
                        act.wait_ge(s_tr, g + i + 1)
                        at = (bi % 2) * 1024 + i * 512
                        group_hi(group_bank(g + i), x_hi[:, at:at + 512])

                branch_hi(0)
                branch_hi(1)
                sp_.upto(base + 30 + 3, end)
                deviation(6 * l + 2, 8)
                sp_.upto(base + 32 + 3, end)
                branch_hi(2)
                sp_.upto(base + 34 + 3, end)
                for i in range(4):
                    g = g_layer + 21 + i
                    act.wait_ge(s_tr, g + 1)
                    group_hi(group_bank(g), x_hi[:, i * 512:i * 512 + 512])
                sp_.upto(end, end)
                act.wait_ge(s_used, end)
                for t in range(NT):
                    square(ps[:, t:4:2, :], t, o_b.rearrange("p (a n) -> p a n", n=N))
                deviation(6 * l + 3)
                norm(2 * l + 1, 6 * l + 4)
                if l == 0:
                    ff(U_FFN, 0, 0, FFN_STEPS, NT)
                    act.wait_ge(s_used, U_MIX1)
                    for t in range(NT):
                        square(banks(4 + 2 * t, 2), t)
                    deviation(5)

            act.wait_ge(s_router, 16)
            nc.scalar.activation(r_hi[:], r_raw, ACT.Copy).then_inc(s_rsp, 1)
            act.wait_ge(s_top, 1)
            nc.scalar.activation(rt[:, 8, 2:4], rt[:, 8, 0:2], ACT.Exp).then_inc(s_tope, 1)

            def hg_hi(n):
                act.wait_ge(s_hg, n)
                nc.scalar.activation(x_hi[:, 0:1024], hg_tmp, ACT.Copy).then_inc(s_hghi, 1)

            act.wait_ge(s_ids, 1)
            items = act.value_load(ids[0:1, 0:1], min_val=0, max_val=MAX_OVER) + N_EXP
            hg_hi(1)
            act.wait_ge(s_yzero, 1)
            nc.scalar.activation(warm[:], ones[:], ACT.Silu)

            def result(n):
                act.wait_ge(s_used, Unit(U_MOE, n * MOE_STEPS).number)
                nc.scalar.activation(y_sb, banks(4, 2), ACT.Copy).then_inc(s_ysb, 1)

            with act.Fori(0, items) as it:
                def weights():
                    act.wait_ge(s_selt, it + 1)
                    nc.scalar.activation(sel_t, banks(3)[:, 0:2 * P], ACT.Copy).then_inc(s_selc, 1)

                ff(U_MOE, it * MOE_STEPS, it * MOE_STEPS + FFN_STEPS, MOE_STEPS, 1,
                   first=lambda: result(it), early=(None, None, None, weights, None),
                   behind=lambda: hg_hi(it + 2))
            result(items)
            act.wait_ge(s_yadd, items * 2 + 2)
            for t in range(NT):
                square(y_acc[:, t * D:t * D + D], t)
            deviation(11)

        @block.vector
        def _(dve):
            ch = Chain(dve, s_dch)
            sp_ = Splits(dve, split_lo)
            v = nc.vector

            def mod_acc_half(q, half, slot=None):
                static = isinstance(q, int)
                if half == 0 and not (static and q < 2):
                    dve.wait_ge(s_mps, q if not static or q == 20 else q - 1)
                acc = mod_acc[:, q % 2 if slot is None else slot, :]
                for k in range(4 * half, 4 * half + 4):
                    s = k % 4
                    if static and q < FIRST_MOD:
                        u = Unit(2 * q + half - MOD_UNITS)
                        if s == 0:
                            dve.wait_ge(s_unit[u.slot], u.landed)
                        src = ring[:, u.slot, s * N:s * N + N]
                    else:
                        dve.wait_ge(s_mod[s // 2], 16 * (2 * q - 2 * FIRST_MOD + half + 1))
                        src = mod_ring[:, s, :]
                    if k == 0:
                        v.tensor_scalar(acc, src, c_col[:, 0:1], None, ALU.mult).then_inc(s_macc, 1)
                    else:
                        dve.wait_ge(s_macc, 8 * q + k)
                        v.scalar_tensor_tensor(out=acc, in0=src, scalar=c_col[:, k:k + 1], in1=acc,
                                               op0=ALU.mult, op1=ALU.add).then_inc(s_macc, 1)

            def mod_take_col(q, index, bank=6):
                dve.wait_ge(s_mps, q + 1)
                v.tensor_copy(index, banks(bank)[:, 0:4].rearrange("p (o j) -> p o j", o=1)).then_inc(s_mev, 1)

            def mod_take(q):
                l, c = MOD[q]
                if c in (4, 5, 10, 11):
                    at = (c // 6) * D + (c % 2) * N
                    dve.wait_ge(s_mps, q + 1)
                    ch.link(v.tensor_copy(g_rows[:, at:at + N], banks(7)))
                    v.tensor_tensor(g_rows[:, at:at + N], banks(6), g_rows[:, at:at + N], ALU.mult).then_inc(s_mev, 1)
                else:
                    mod_take_col(q, mod_col[:, l * 12 + c:l * 12 + c + 1, :])

            def columns(l, which, taken):
                dve.wait_ge(s_mev, taken)
                for half in range(2):
                    sc, sh = l * 12 + 6 * which + 2 + half, l * 12 + 6 * which + half
                    gain = R_NORM + (l * 4 + 2 * which) * 2 + half
                    j = slice(4 * half, 4 * half + 4)
                    ch.link(v.tensor_tensor(col_tmp[:], mod_col[:, sc, :], row_cols[:, :, sc], ALU.add))
                    ch.link(v.scalar_tensor_tensor(out=s_col[:, j], in0=col_tmp[:], scalar=1.0,
                                                   in1=row_cols[:, :, gain], op0=ALU.add, op1=ALU.mult))
                    ch.link(v.tensor_tensor(b_col[:, j], mod_col[:, sh, :], row_cols[:, :, sh], ALU.add))

            def rstd(r, squares, n, width):
                if squares:
                    dve.wait_ge(s_sq, squares)
                v.tensor_scalar(var[:, 0:n], ssq[:, 0:n], 1.0 / width, EPS, ALU.mult, ALU.add).then_inc(s_var, 1)
                dve.wait_ge(s_sd, r + 1)
                ch.link(v.reciprocal(rs[:, 0:n], sd[:, 0:n]))

            def norm(n, g0):
                for t in range(NT):
                    v.tensor_scalar(xhat[:, t * D:t * D + D], x[:, t * D:t * D + D], rs[:, t:t + 1], None, ALU.mult) \
                        .then_inc(s_xhat, 1)

                def scaled(i):
                    dve.wait_ge(s_tr, g0 + i + 1)
                    for k in range(2):
                        ins = v.tensor_scalar(h_tmp[:, i % 2, k * SEQ:k * SEQ + SEQ],
                                              group_bank(g0 + i)[:, k * SEQ:k * SEQ + SEQ],
                                              s_col[:, 2 * i + k:2 * i + k + 1], b_col[:, 2 * i + k:2 * i + k + 1],
                                              ALU.mult, ALU.add)
                    ins.then_inc(s_tmp, 1)

                def low(i):
                    dve.wait_ge(s_tmp, 4 * n + i + 1)
                    hi = 18 * (n // 2) + (0 if n % 2 == 0 else 14) + i + 1
                    dve.wait_ge(s_ghi, hi)
                    w = slice(i * 512, i * 512 + 512)
                    v.tensor_tensor(x_lo[:, w], h_tmp[:, i % 2, :], x_hi[:, w].bitcast(F32), ALU.subtract) \
                        .then_inc(s_free, 1)

                scaled(0)
                scaled(1)
                low(0)
                scaled(2)
                low(1)
                scaled(3)
                low(2)
                low(3)

            def residual(n, y):
                gr = g_rows[:, (n % 2) * D:(n % 2) * D + D]
                for t in range(NT):
                    src = y(t)
                    if len(src.shape) == 3:
                        tmp, g3 = o_b.rearrange("p (a n) -> p a n", n=N), gr.rearrange("p (a n) -> p a n", n=N)
                    else:
                        tmp, g3 = o_b, gr
                    if t:
                        dve.wait_ge(s_xupd, NT * n + t)
                    ch.link(v.scalar_tensor_tensor(out=tmp, in0=src, scalar=rs[:, t:t + 1], in1=g3,
                                                   op0=ALU.mult, op1=ALU.mult))
                    xt = x[:, t * D:t * D + D]
                    v.tensor_tensor(xt, xt, o_b, ALU.add).then_inc(s_xupd, 1)

            def ff(base, d0, f0, steps, nt, mod_steps=0, first=None, early=(), behind=None):
                def mult(j):
                    dve.wait_ge(s_fsilu, f0 + j + 1)
                    s3 = silu_buf.rearrange("p (t n) -> p t n", n=FF)[:, 0:nt, :]
                    a3 = act_buf.rearrange("p (t n) -> p t n", n=FF)[:, 0:nt, :]
                    v.tensor_tensor(a3, s3, ps[:, 0:nt, FF:2 * FF], ALU.mult).then_inc(s_fact, 1)

                def act_lo(j):
                    dve.wait_ge(s_fhi, f0 + j + 1)
                    w = 2 * nt * P
                    v.tensor_tensor(a_lo[:, 0:w], banks(2)[:, 0:w], a_hi[:, 0:w].bitcast(F32), ALU.subtract) \
                        .then_inc(s_flo, 1)

                def step(j):
                    split_lo(dve, Unit(base + 2, d0 + j))
                    mult(j)
                    split_lo(dve, Unit(base + 3, d0 + j))
                    act_lo(j)
                    split_lo(dve, Unit(base + 4, d0 + j))

                split_lo(dve, Unit(base, d0))
                split_lo(dve, Unit(base + 1, d0))
                if first:
                    first()
                if mod_steps:
                    with dve.Fori(0, mod_steps) as j:
                        mod_acc_half(j + 12, 0, 0)
                        mod_acc_half(j + 12, 1, 0)
                        step(j)
                        mod_take_col(j + 12, mod_col[:, bass.ds(j + (j // 4) * 2 + 12, 1), :], 3)
                    with dve.Fori(mod_steps, steps - 1) as j:
                        step(j)
                else:
                    for j, extra in enumerate(early):
                        step(j)
                        if extra:
                            extra()
                    with dve.Fori(len(early), steps - 1) as j:
                        step(j)
                last = steps - 1
                split_lo(dve, Unit(base + 2, d0 + last))
                mult(last)
                act_lo(last)
                if behind:
                    behind()

            dve.wait_ge(s_tr, 2)
            v.tensor_copy(row_cols[:].rearrange("p j r -> p (j r)"), banks(5)[:, 0:4 * N_ROWS]).then_inc(s_free, 1)
            dve.wait_ge(s_cs, 1)
            dve.wait_ge(s_free, 1)
            for q in range(FIRST_MOD):
                mod_acc_half(q, 0)
                mod_acc_half(q, 1)
                if q > 0:
                    mod_take(q - 1)
            mod_take(FIRST_MOD - 1)

            for l in range(DEPTH):
                base = l * U_MIX1
                end = base + MIX_UNITS
                g_layer = 2 + l * G_LAYER
                gw = g_layer + 4
                sp_.n = base
                hi0 = 18 * l

                columns(l, 0, 4 if l == 0 else 20)
                sp_.upto(base + 2, end)
                rstd(6 * l, 8 * l + 2, 2, D)
                norm(2 * l, g_layer)

                if l == 0:
                    ch.link(v.memset(lb_row, 0.0))
                    ch.link(v.memset(om_row, float(P) ** -0.5))
                else:
                    dve.wait_ge(s_lb, 16)
                    ch.link(v.tensor_tensor(lb_row, o_b[:, 0:512], o_b[:, 512:1024], ALU.max))
                    ob3 = o_b.rearrange("p (l n) -> p l n", n=512)
                    v.tensor_tensor(ob3, ob3, lb_row[:, None, :].to_broadcast([P, 2, 512]), ALU.subtract) \
                        .then_inc(s_lbd, 1)
                    dve.wait_ge(s_lbe, 1)
                    ch.link(v.tensor_tensor(om_row, o_b[:, 0:512], o_b[:, 512:1024], ALU.add))
                    ch.link(v.reciprocal(om_row, om_row))
                    ch.link(v.tensor_tensor(lb_row, o_b[:, 512:1024], om_row, ALU.mult))
                    ch.link(v.tensor_scalar(om_row, lb_row, -1.0, 1.0, ALU.mult, ALU.add))
                    ch.link(v.tensor_scalar(om_row, om_row, float(P) ** -0.5, None, ALU.mult))
                lb3 = lb_row[:, None, :].to_broadcast([P, NT, 512])
                om3 = om_row[:, None, :].to_broadcast([P, NT, 512])

                def t3(ap):
                    return ap.rearrange("p (t n) -> p t n", t=NT)

                def take_group(i, block):
                    dve.wait_ge(s_tr, gw + i + 1)
                    v.tensor_copy(ft[:, block * SEQ:block * SEQ + 512], group_bank(gw + i)).then_inc(s_free, 1)

                for c in range(N_WIN + 1):
                    if c == 1:
                        dve.wait_ge(s_eva, 30 * l + 2)
                        if l == 1:
                            dve.wait_ge(s_park, 16)
                        v.tensor_scalar(gate_g, stage_f, -1.0, 40.0, ALU.mult, ALU.min).then_inc(s_f1, 1)
                    if c == 2:
                        dve.wait_ge(s_kc, l + 1)
                        v.tensor_tensor(t3(stage_k), t3(stage_k), om3, ALU.mult).then_inc(s_kr, 1)
                        dve.wait_ge(s_f2, l + 1)
                        v.tensor_tensor(t3(gate_g), t3(gate_g), lb3, ALU.mult).then_inc(s_f3, 1)
                    if c == 3:
                        take_group(0, 10)
                        take_group(1, 12)
                        dve.wait_ge(s_f4, 2 * l + 2)
                        ch.link(v.scalar_tensor_tensor(out=log_f, in0=stage_f, scalar=0.0, in1=gate_h,
                                                       op0=ALU.min, op1=ALU.subtract))
                        ch.link(v.tensor_tensor(log_f, log_f, gate_g, ALU.add))
                        ch.link(v.tensor_scalar(v_h, stage_f, 40.0, 0.0, ALU.add, ALU.min))
                        ch.link(v.scalar_tensor_tensor(out=t3(v_h), in0=lb3, scalar=0.0, in1=t3(v_h),
                                                       op0=ALU.is_gt, op1=ALU.mult))
                        v.tensor_tensor(log_f, log_f, v_h, ALU.subtract).then_inc(s_logf, 1)
                    if c == 4:
                        take_group(2, 14)
                        take_group(3, 16)
                        take_group(4, 6)
                        take_group(5, 8)
                    if c == 5:
                        dve.wait_ge(s_tr, gw + 7)
                        v.tensor_copy(glr_t[0:16, :], group_bank(gw + 6)[0:16, 0:SEQ]).then_inc(s_free, 1)
                        take_group(7, 4)
                    if c == 6:
                        take_group(8, 0)
                        take_group(9, 2)
                        dve.wait_ge(s_tr, gw + 11)
                        dve.wait_ge(s_la, l + 1)
                        ch.link(v.scalar_tensor_tensor(out=log_a, in0=group_bank(gw + 10), scalar=0.0,
                                                       in1=stage_q[:, 0:512], op0=ALU.min, op1=ALU.subtract))
                        v.tensor_scalar(log_a, log_a, 1.0 / 16.0, None, ALU.mult).then_inc(s_free, 1)
                    q = mod_of_win(l, c - 2) if c > 1 else None
                    if q is not None:
                        mod_take(q)
                    q = mod_of_win(l, c) if c < N_WIN else None
                    for half in range(2):
                        sp_.upto(min(base + 2 * c + 3 + half, base + 2 * N_WIN + 3), end)
                        if q is not None:
                            mod_acc_half(q, half)

                dve.wait_ge(s_par, 16 * 5)
                dve.wait_ge(s_gain, 32 * (l + 1))

                def swa_max(i):
                    g, t = i // 2, i % 2
                    w = P * (t + 1)
                    dve.wait_ge(s_ss, 4 * l + i + 1)
                    dist = tb[:, B_DIST + P * t:B_DIST + P * t + w]
                    for h in range(4):
                        slope = 2.0 ** -(4 * g + h + 1)
                        ins = v.scalar_tensor_tensor(out=e_buf[:, h * 256:h * 256 + w], in0=dist, scalar=-slope,
                                                     in1=swa_bank(h)[:, 0:w], op0=ALU.mult, op1=ALU.add)
                    ins.then_inc(s_sst, 1)
                    dve.wait_ge(s_sst, 4 * l + i + 1)
                    sink = sinks[:, l * 8 + 4 * g:l * 8 + 4 * g + 4]
                    ch.link(v.tensor_reduce(soft[:, 0, :], e_buf.rearrange("p (h w) -> p h w", w=256)[:, :, 0:w],
                                            AX.X, ALU.max))
                    ch.link(v.tensor_tensor(soft[:, 0, :], soft[:, 0, :], sink, ALU.max))
                    ch.link(v.tensor_scalar(soft[:, 1, :], soft[:, 0, :], -1.0, None, ALU.mult))
                    v.tensor_tensor(soft[:, 2, :], sink, soft[:, 0, :], ALU.subtract).then_inc(s_nm, 1)

                def swa_taken(i):
                    g, t = i // 2, i % 2
                    dve.wait_ge(s_so, 4 * l + i + 1)
                    for h in range(4):
                        at = t * N + (4 * g + h) * 64
                        ins = v.tensor_scalar(o_b[:, at:at + 64], banks(3)[:, h * 64:h * 64 + 64],
                                              rden[:, i % 2, h:h + 1], None, ALU.mult)
                    ins.then_inc(s_soe, 1)

                swa_max(0)
                for i in range(4):
                    dve.wait_ge(s_pr, 4 * l + i + 1)
                    ch.link(v.tensor_tensor(soft[:, 5, :], soft[:, 3, :], soft[:, 4, :], ALU.add))
                    ch.link(v.reciprocal(rden[:, i % 2, :], soft[:, 5, :]))
                    if i < 3:
                        swa_max(i + 1)
                    sp_.upto(base + 2 * N_WIN + i + 3, end)
                    swa_taken(i)

                def queries(i):
                    kind, n, t = ARGS[i]
                    dve.wait_ge(s_exp, NA * l + i + 1)
                    if i > 0:
                        dve.wait_ge(s_sc, NR * l + rounds_before(i))
                    lv = 7 + t
                    ev = e_buf.rearrange("p (v n) -> p v n", n=P)[:, 0:lv, :]
                    qv = q_buf.rearrange("p (v n) -> p v n", n=P)[:, 0:lv, :]
                    v.tensor_tensor(qv, ev, q_block(kind, n, t)[:, None, :].to_broadcast([P, lv, P]), ALU.mult)
                    rest = slice(t + POOL_LEVELS, t + N_LEVELS)
                    v.tensor_tensor(k_buf.rearrange("p (v n) -> p v n", n=P)[:, rest, :],
                                    e_buf.rearrange("p (v n) -> p v n", n=P)[:, rest, :],
                                    k_block(kind, n, t)[:, None, :].to_broadcast([P, N_LEVELS - POOL_LEVELS, P]),
                                    ALU.mult).then_inc(s_qe, 1)

                def mask(r):
                    dve.wait_ge(s_sc, NR * l + r + 1)
                    if r > 0:
                        dve.wait_ge(s_psum, NR * l + r)
                    v.tensor_tensor(p_buf, banks(6, 2), tb[:, B_MASK:B_MASK + 1024], ALU.mult).then_inc(s_mask, 1)

                def reduce(r):
                    dve.wait_ge(s_mask, NR * l + r + 1)
                    if r > 1:
                        dve.wait_ge(s_o, NR * l + r - 1)
                    v.tensor_reduce(p_sum[:, (r % 2) * P:(r % 2) * P + P], p_buf.rearrange("p (v n) -> p n v", n=P),
                                    AX.X, ALU.add).then_inc(s_psum, 1)

                def heads(o, gate, which):
                    dve.wait_ge(s_oe, NR * l + (8 if which == 0 else NR))
                    dve.wait_ge(s_psum, NR * l + (rounds_before(HEADS_STEP + 1) if which == 0 else NR))
                    o3 = o.rearrange("p (b e) -> p b e", e=P)
                    ch.link(v.tensor_tensor(p_buf, o, o, ALU.mult))
                    ch.link(v.tensor_reduce(ssq[:, 0:8], p_buf.rearrange("p (b e) -> p b e", e=P), AX.X, ALU.add))
                    rstd(6 * l + 1 + which, 0, 8, P)
                    gain = head_gain[:, which * P:which * P + P]
                    ch.link(v.tensor_tensor(o3, o3, rs[:, 0:8][:, :, None].to_broadcast([P, 8, P]), ALU.mult))
                    ch.link(v.tensor_tensor(o3, o3, gain[:, None, :].to_broadcast([P, 8, P]), ALU.mult))
                    v.tensor_tensor(o, o, gate, ALU.mult).then_inc(s_heads, 1)

                queries(0)
                for i in range(NA):
                    mine = [r for r, (q, _) in enumerate(ROUNDS) if q == i]
                    for r in mine:
                        mask(r)
                        if r == mine[-1] and i + 1 < NA:
                            queries(i + 1)
                        reduce(r)
                    if i == HEADS_STEP:
                        heads(o_a, gate_g, 0)
                    if i < 7:
                        sp_.upto(base + 2 * N_WIN + 4 + i + 3, end)

                def low_group(g, hi, at):
                    dve.wait_ge(s_ghi, hi0 + hi + 1)
                    v.tensor_tensor(x_lo[:, at:at + 512], group_bank(g), x_hi[:, at:at + 512].bitcast(F32),
                                    ALU.subtract).then_inc(s_free, 1)

                def branch_low(bi):
                    for i in range(2):
                        low_group(g_layer + 15 + 2 * bi + i, 4 + 2 * bi + i, (bi % 2) * 1024 + i * 512)

                def gated(bi):
                    b = BRANCHES[bi]
                    for n in range(2):
                        c = 15 + 2 * bi + n
                        dve.wait_ge(s_used, base + 30 + 2 * bi + n + 1)
                        if bi == 0 and n == 0:
                            dve.wait_ge(s_eva, 30 * l + 30)
                        for t in range(NT):
                            m = merged[:, t * D + n * N:t * D + n * N + N]
                            src = ps[:, pair(c) + t, :]
                            gate = merge_gate(2 * b + n, t)
                            if bi == 0:
                                v.tensor_tensor(m, src, gate, ALU.mult).then_inc(s_evd, 1)
                            else:
                                tmp = p_buf[:, t * N:t * N + N]
                                v.tensor_tensor(tmp, src, gate, ALU.mult).then_inc(s_evd, 1)
                                dve.wait_ge(s_evd, 12 * l + 4 * bi + 2 * n + t + 1)
                                ins = v.tensor_tensor(m, m, tmp, ALU.add)
                                if bi == 2:
                                    ins.then_inc(s_merged, 1)
                                else:
                                    ch.link(ins)

                branch_low(0)
                branch_low(1)
                sp_.upto(base + 30 + 3, end)
                heads(o_c, gate_h, 1)
                gated(0)
                sp_.upto(base + 32 + 3, end)
                branch_low(2)
                gated(1)
                sp_.upto(base + 34 + 3, end)
                gated(2)
                for i in range(4):
                    low_group(g_layer + 21 + i, 10 + i, i * 512)
                sp_.upto(end, end)
                rstd(6 * l + 3, 8 * l + 4, 2, D)
                dve.wait_ge(s_xre, 16 * (l + 1))
                residual(2 * l, lambda t: ps[:, t:4:2, :])
                columns(l, 1, 10 if l == 0 else 20)
                rstd(6 * l + 4, 8 * l + 6, 2, D)
                norm(2 * l + 1, g_layer + 25)
                if l == 0:
                    ff(U_FFN, 0, 0, FFN_STEPS, NT, mod_steps=8)
                    rstd(5, 8, 2, D)
                    residual(1, lambda t: banks(4 + 2 * t, 2))

            dve.wait_ge(s_rsp, 1)
            v.tensor_tensor(r_lo[:], r_raw, r_hi[:].bitcast(F32), ALU.subtract).then_inc(s_rsp, 1)
            v.memset(y_acc, 0.0)
            v.memset(sel_t, 0.0).then_inc(s_selc, 1)
            lg, eq, one1, lg2, one2, wsel, mem_, pos_m = [rt[:, i, :].rearrange("p (t e) -> p t e", e=N_EXP) for i in range(8)]
            small = rt[:, 9, :]
            rev = rt[:, 10, 0:8]
            over, rank, hot = rt[:, 10, 8:16], rt[:, 11, 0:8], rt[:, 11, 8:16]
            idf = rt[:, 13, 0:4]
            hots = work[:, 1024:1024 + 8 * MAX_OVER].rearrange("p (r e) -> p r e", e=N_EXP)
            prods = work[:, 1088:1088 + 8 * MAX_OVER].rearrange("p (r e) -> p r e", e=N_EXP)
            iota = tb[:, B_IOTA:B_IOTA + P]

            def bc(col):
                return col[:, :, None].to_broadcast([P, NT, N_EXP])

            mch = Chain(dve, s_mdch)

            def current(i):
                mch.link(v.tensor_copy(cur[:, 0:2].rearrange("p (o t) -> p o t", o=1), pos_items[:, bass.ds(i, 1), :]))
                mch.link(v.tensor_copy(cur[:, 2:4].rearrange("p (o t) -> p o t", o=1), w_items[:, bass.ds(i, 1), :]))

            def select():
                for t in range(NT):
                    ins = v.tensor_scalar(sel[:, t * P:t * P + P], iota, cur[:, t:t + 1], None, ALU.is_equal)
                ins.then_inc(s_sel, 1)

            ch.link(v.tensor_scalar(rev, iota[:, 0:8], -1.0, 8.0, ALU.mult, ALU.add))
            dve.wait_ge(s_logit, 1)
            v.tensor_copy(logit_rows, banks(6)[0:N_EXP, 0:SEQ]).then_inc(s_lrow, 1)
            dve.wait_ge(s_logit, 2)
            ch.link(v.tensor_copy(rt[:, 0, :], banks(7)[:, 0:16]))

            def choose(src, one, m):
                ch.link(v.tensor_reduce(small[:, m:m + 2], src, AX.X, ALU.max))
                ch.link(v.tensor_tensor(eq, src, bc(small[:, m:m + 2]), ALU.is_equal))
                ch.link(v.tensor_tensor(eq, eq, rev[:, None, :].to_broadcast([P, NT, N_EXP]), ALU.mult))
                ch.link(v.tensor_reduce(small[:, 4:6], eq, AX.X, ALU.max))
                ch.link(v.tensor_tensor(one, eq, bc(small[:, 4:6]), ALU.is_equal))

            choose(lg, one1, 0)
            ch.link(v.scalar_tensor_tensor(out=rt[:, 3, :], in0=rt[:, 2, :], scalar=-3.0e38, in1=rt[:, 0, :],
                                           op0=ALU.mult, op1=ALU.add))
            choose(lg2, one2, 2)
            ch.link(v.tensor_tensor(rt[:, 6, :], rt[:, 2, :], rt[:, 4, :], ALU.add))
            v.tensor_copy(m_bf[:], rt[:, 6, :]).then_inc(s_m, 1)
            v.tensor_tensor(rt[:, 8, 0:2], small[:, 2:4], small[:, 0:2], ALU.subtract).then_inc(s_top, 1)
            dve.wait_ge(s_tope, 1)
            ch.link(v.tensor_scalar(small[:, 6:8], rt[:, 8, 2:4], 1.0, None, ALU.add))
            ch.link(v.reciprocal(small[:, 8:10], small[:, 6:8]))
            ch.link(v.tensor_tensor(small[:, 10:12], small[:, 8:10], rt[:, 8, 2:4], ALU.mult))
            ch.link(v.tensor_tensor(one1, one1, bc(small[:, 8:10]), ALU.mult))
            ch.link(v.tensor_tensor(one2, one2, bc(small[:, 10:12]), ALU.mult))
            ch.link(v.tensor_tensor(wsel, one1, one2, ALU.add))
            dve.wait_ge(s_pos, 1)
            ch.link(v.tensor_scalar(rt[:, 7, :], banks(7)[:, 0:16], 1.0, None, ALU.add))
            ch.link(v.tensor_tensor(rt[:, 7, :], rt[:, 7, :], rt[:, 6, :], ALU.mult))
            ch.link(v.tensor_scalar(rt[:, 7, :], rt[:, 7, :], -1.0, None, ALU.add))
            ch.link(v.memset(gate_g[:, 776:824], 0.0))
            for t in range(NT):
                ch.link(v.tensor_copy(pos_items[:, 0:8, t], pos_m[:, t, :]))
                ch.link(v.tensor_copy(w_items[:, 0:8, t], wsel[:, t, :]))
            ch.link(v.tensor_scalar(over, banks(7)[:, 16:24], float(P), None, ALU.is_gt))
            current(0)
            select()
            ch.link(v.memset(rt[:, 11:16, :], 0.0))
            ch.link(v.tensor_copy(rank[:, 1:8], over[:, 0:7]))
            for shift in (1, 2, 4):
                a_, b_ = (rank, hot) if shift != 2 else (hot, rank)
                ch.link(v.tensor_tensor(b_[:, shift:8], a_[:, shift:8], a_[:, 0:8 - shift], ALU.add))
                ch.link(v.tensor_copy(b_[:, 0:shift], a_[:, 0:shift]))
            ch.link(v.tensor_tensor(idf[:, 0:1], hot[:, 7:8], over[:, 7:8], ALU.add))
            ch.link(v.tensor_scalar(rt[:, 7, :], rt[:, 7, :], -float(P), None, ALU.add))
            for i in range(MAX_OVER):
                ch.link(v.scalar_tensor_tensor(out=hots[:, i, :], in0=hot, scalar=float(i), in1=over,
                                               op0=ALU.is_equal, op1=ALU.mult))
            ch.link(v.tensor_tensor(prods, hots, iota[:, None, 0:8].to_broadcast([P, MAX_OVER, N_EXP]), ALU.mult))
            ch.link(v.tensor_reduce(idf[:, 1:1 + MAX_OVER], prods, AX.X, ALU.add))
            for t in range(NT):
                for table, source in ((pos_items, pos_m), (w_items, wsel)):
                    ch.link(v.tensor_tensor(prods, hots, source[:, t, None, :].to_broadcast([P, MAX_OVER, N_EXP]),
                                            ALU.mult))
                    ch.link(v.tensor_reduce(table[:, 8:8 + MAX_OVER, t], prods, AX.X, ALU.add))
            v.tensor_copy(ids[:], idf[0:1, :]).then_inc(s_ids, 1)

            def gathered(n):
                dve.wait_ge(s_gat, n)
                for k in range(KD):
                    ins = v.tensor_scalar(hg_tmp[:, k * P:k * P + P], banks(6, 2)[:, k * P:k * P + P],
                                          s_col[:, k:k + 1], b_col[:, k:k + 1], ALU.mult, ALU.add)
                ins.then_inc(s_hg, 1)

            def gathered_low(n):
                dve.wait_ge(s_hghi, n)
                v.tensor_tensor(x_lo[:, 0:1024], hg_tmp, x_hi[:, 0:1024].bitcast(F32), ALU.subtract) \
                    .then_inc(s_hglo, 1)

            def add_rows(n, t, bank):
                dve.wait_ge(s_scat, 2 * n + t + 1)
                y = y_acc[:, t * D:t * D + D]
                v.tensor_tensor(y, y, banks(bank, 2), ALU.add).then_inc(s_yadd, 1)

            gathered(1)
            gathered_low(1)
            dve.wait_ge(s_ids, 1)
            items = dve.value_load(ids[0:1, 0:1], min_val=0, max_val=MAX_OVER) + N_EXP
            with dve.Fori(0, items) as it:
                mch.base = it * 2

                def first():
                    for t in range(NT):
                        ins = v.tensor_scalar(sel_w[:, t * P:t * P + P], iota, cur[:, t:t + 1], cur[:, 2 + t:3 + t],
                                              ALU.is_equal, ALU.mult)
                    ins.then_inc(s_selw, 1)
                    dve.wait_ge(s_selw, it + 1)
                    current(it + 1)
                    select()

                ff(U_MOE, it * MOE_STEPS, it * MOE_STEPS + FFN_STEPS, MOE_STEPS, 1, first=first,
                   early=(lambda: add_rows(it, 0, 6), None, lambda: add_rows(it, 1, 6), None,
                          lambda: gathered(it + 2)),
                   behind=lambda: gathered_low(it + 2))
            add_rows(items, 0, 6)
            add_rows(items, 1, 4)
            rstd(11, 16, 2, D)
            residual(3, lambda t: y_acc[:, t * D:t * D + D])

        @block.tensor
        def _(pe):
            t_ = nc.tensor

            def row(r):
                return ident[0:N_ROWS, r:r + 1].to_broadcast([N_ROWS, P])

            def mod_sum_col(q, bank=6, slot=0):
                pe.wait_ge(s_macc, 8 * q + 8)
                if not (isinstance(q, int) and q == 0):
                    pe.wait_ge(s_mev, q)
                for j in range(4):
                    mm = t_.matmul(banks(bank)[:, j:j + 1], mod_acc[:, slot, j * P:j * P + P], ones[:], start=True, stop=True)
                mm.then_inc(s_mps, 1)

            def mod_sum(q):
                l, c = MOD[q]
                if c not in (4, 5, 10, 11):
                    mod_sum_col(q, slot=q % 2)
                    return
                pe.wait_ge(s_mev, q)
                gain = R_NORM + (l * 4 + (1 if c < 6 else 3)) * 2 + c % 2
                t_.matmul(banks(7), row(gain), rows[:], start=True, stop=True)
                t_.matmul(banks(6), row(R_BMOD + 12 * l + c), rows[:], start=True, stop=False)
                pe.wait_ge(s_macc, 8 * q + 8)
                t_.matmul(banks(6), ones[:].to_broadcast([P, P]), mod_acc[:, q % 2, :], start=False, stop=True) \
                    .then_inc(s_mps, 1)

            def turn_group(g, blocks):
                if g >= 3:
                    pe.wait_ge(s_free, g - 2)
                for i, src in enumerate(blocks):
                    mm = t_.transpose(group_bank(g)[:, i * P:i * P + P], src, ident)
                mm.then_inc(s_tr, 1)

            def norm_groups(n, g0):
                pe.wait_ge(s_xhat, (n + 1) * NT)
                for i in range(4):
                    turn_group(g0 + i, [xhat[:, t * D + k * P:t * D + k * P + P] for k in (2 * i, 2 * i + 1)
                                        for t in range(NT)])

            def stage_groups(g, stage, width=N):
                for i in range(width // 256):
                    turn_group(g + i, [stage[:, t * N + k * P:t * N + k * P + P] for k in (2 * i, 2 * i + 1)
                                       for t in range(NT)])

            def ff(base, d0, f0, steps, nt, left, mod_steps=0, first=None, early=()):
                def up(j, u0, u1):
                    pe.wait_ge(s_fact, f0 + j)
                    acc = [ps[:, t, :] for t in range(nt)]
                    product(pe, u0, left, acc, N, True, False, 0, nt)
                    product(pe, u1, left, acc, N, False, True, 4, nt)

                def turn(j):
                    pe.wait_ge(s_fact, f0 + j + 1)
                    pe.wait_ge(s_flo, f0 + j)
                    for k in range(2):
                        for t in range(nt):
                            at = (k * nt + t) * P
                            mm = t_.transpose(banks(2)[:, at:at + P], act_buf[:, t * FF + k * P:t * FF + k * P + P], ident)
                    mm.then_inc(s_ftr, 1)

                def down(j, u):
                    pe.wait_ge(s_flo, f0 + j + 1)
                    pe.wait_ge(s_lo, u.number + 1)
                    wh = w_hi[:, u.slot, :].rearrange("p (k n) -> p k n", n=D)
                    wl = w_lo[:, u.slot, :].rearrange("p (k n) -> p k n", n=D)
                    for k in range(2):
                        for t in range(nt):
                            at = (k * nt + t) * P
                            hi, lo = a_hi[:, at:at + P], a_lo[:, at:at + P]
                            for n in range(2):
                                for lhs, rhs in ((hi, wh), (hi, wl), (lo, wh)):
                                    mm = t_.matmul(ps[:, 4 + 2 * t + n, :], lhs, rhs[:, k, n * N:n * N + N],
                                                   start=False, stop=False, skip_group_check=True)
                    mm.then_inc(s_used, 1)

                up(0, Unit(base, d0), Unit(base + 1, d0))
                if first:
                    first()
                for b in range(4, 4 + 2 * nt):
                    t_.matmul(ps[:, b, :], tb[:, B_ZERO:B_ZERO + P], tb[:, B_MASK:B_MASK + N], start=True, stop=False,
                              skip_group_check=True)
                turn(0)

                def step(j, extra=None):
                    up(j + 1, Unit(base + 2, d0 + j), Unit(base + 3, d0 + j))
                    down(j, Unit(base + 4, d0 + j))
                    if extra:
                        extra()
                    turn(j + 1)

                if mod_steps:
                    with pe.Fori(0, mod_steps) as j:
                        mod_sum_col(j + 12, 3)
                        step(j)
                    with pe.Fori(mod_steps, steps - 1) as j:
                        step(j)
                else:
                    for j, extra in enumerate(early):
                        step(j, extra)
                    with pe.Fori(len(early), steps - 1) as j:
                        step(j)
                down(steps - 1, Unit(base + 2, d0 + (steps - 1)))

            pe.wait_ge(s_const, 17)
            pe.wait_ge(s_c, 16)
            t_.transpose(banks(4)[:, 0:KD], c_rows[:], ident[0:KD, 0:KD]).then_inc(s_tr, 1)
            pe.wait_ge(s_rows, 48)
            for j in range(4):
                mm = t_.transpose(banks(5)[:, j * N_ROWS:j * N_ROWS + N_ROWS], rows[:, j * P:j * P + P],
                                  ident[0:N_ROWS, 0:N_ROWS])
            mm.then_inc(s_tr, 1)
            for q in range(FIRST_MOD):
                mod_sum(q)

            for l in range(DEPTH):
                base = l * U_MIX1
                g_layer = 2 + l * G_LAYER
                gw = g_layer + 4
                if l == 0:
                    pe.wait_ge(s_cs, 1)
                norm_groups(2 * l, g_layer)
                pe.wait_ge(s_free, g_layer - 1 + 2)

                for c in range(N_WIN):
                    if c >= 2:
                        pe.wait_ge(s_eva, 30 * l + 2 * (c - 1))
                    width = W_IN_CHUNKS[c][1]
                    acc = [ps[:, pair(c) + t, 0:width] for t in range(NT)]
                    product(pe, Unit(base + 2 * c), model_left, acc, width, True, False, 0)
                    if c == 0:
                        pe.wait_ge(s_free, g_layer - 1 + 4)
                    product(pe, Unit(base + 2 * c + 1), model_left, acc, width, False, True, 4)
                    if c == 2:
                        pe.wait_ge(s_eva, 30 * l + 4)
                        stage_groups(gw, stage_q)
                    if c == 3:
                        pe.wait_ge(s_kr, l + 1)
                        stage_groups(gw + 2, stage_k)
                        pe.wait_ge(s_eva, 30 * l + 6)
                        stage_groups(gw + 4, stage_g)
                    if c == 4:
                        pe.wait_ge(s_eva, 30 * l + 8)
                        pe.wait_ge(s_free, gw + 6 - 2)
                        for t in range(NT):
                            mm = t_.transpose(group_bank(gw + 6)[0:16, t * P:t * P + P], misc[:, t * 272:t * 272 + 16], ident)
                        mm.then_inc(s_tr, 1)
                        pe.wait_ge(s_swap, 4 * l + 4)
                        turn_group(gw + 7, [misc[:, t * 272 + 16:t * 272 + 144] for t in range(NT)] +
                                   [sk_swap[:, t * P:t * P + P] for t in range(NT)])
                    if c == 5:
                        pe.wait_ge(s_eva, 30 * l + 10)
                        stage_groups(gw + 8, stage_f)
                        if l == 0:
                            pe.wait_ge(s_par, 16 * 5)
                        pe.wait_ge(s_free, gw + 10 - 2)
                        for t in range(NT):
                            mm = t_.matmul(group_bank(gw + 10)[:, t * 256:t * 256 + 256], glr_t[:, t * P:t * P + P],
                                           gate_w[:, l, :], start=True, stop=True)
                        mm.then_inc(s_tr, 1)
                    q = mod_of_win(l, c - 1) if c > 0 else None
                    if q is not None:
                        mod_sum(q)

                def merge(k):
                    m = k // 2
                    if k % 2 == 0:
                        pe.wait_ge(s_eva, 30 * l + 2 * (N_WIN + m))
                        for t in range(NT):
                            t_.matmul(ps[:, t, :], row(R_MERGE + 6 * l + m), rows[:], start=True, stop=False,
                                      skip_group_check=True)
                    product(pe, Unit(base + 2 * N_WIN + k), model_left, [ps[:, t, :] for t in range(NT)], N,
                            False, k % 2 == 1, 4 * (k % 2))

                def swa_scores(i):
                    g, t = i // 2, i % 2
                    if i == 0:
                        pe.wait_ge(s_free, gw + 10)
                        pe.wait_ge(s_mev, 12 if l == 0 else 24)
                    else:
                        pe.wait_ge(s_sst, 4 * l + i)
                    for h in range(4):
                        half = slice(64 * (h % 2), 64 * (h % 2) + 64)
                        q = ft_block((4 * g + h) // 2, t)[half, :]
                        k = ft_block(4 if h % 2 == g else 5)[half, 0:P * (t + 1)]
                        mm = t_.matmul(swa_bank(h)[:, 0:P * (t + 1)], q, k, start=True, stop=True)
                    mm.then_inc(s_ss, 1)

                def swa_turn(i):
                    t = i % 2
                    pe.wait_ge(s_pr, 4 * l + i + 1)
                    if i > 0:
                        pe.wait_ge(s_pt, 4 * l + i)
                    for h in range(4):
                        for kb in range(t + 1):
                            at = (h * (t + 1) + kb) * P
                            mm = t_.transpose(banks(6, 2)[:, at:at + P], q_buf[:, h * 256 + kb * P:h * 256 + kb * P + P],
                                              ident)
                    mm.then_inc(s_st, 1)

                def swa_out(i):
                    g, t = i // 2, i % 2
                    pe.wait_ge(s_pt, 4 * l + i + 1)
                    if i > 0:
                        pe.wait_ge(s_soe, 4 * l + i)
                    for h in range(4):
                        for kb in range(t + 1):
                            at = (h * (t + 1) + kb) * P
                            val = misc[:, kb * 272 + 144 + g * 64:kb * 272 + 144 + g * 64 + 64]
                            mm = t_.matmul(banks(3)[:, h * 64:h * 64 + 64], k_buf[:, at:at + P], val,
                                           start=kb == 0, stop=kb == t)
                    mm.then_inc(s_so, 1)

                swa_scores(0)
                for i in range(4):
                    merge(i)
                    swa_turn(i)
                    if i < 3:
                        swa_scores(i + 1)
                    swa_out(i)

                def args(i):
                    kind, n, t = ARGS[i]
                    if i > 0:
                        pe.wait_ge(s_exp, NA * l + i)
                    else:
                        pe.wait_ge(s_sst, 4 * l + 4)
                        pe.wait_ge(s_free, gw + 10)
                    if kind == "G":
                        log = log_a[:, t * 256 + n * P:t * 256 + n * P + P]
                    else:
                        log = log_f[:, t * 512 + n * P:t * 512 + n * P + P]
                    col = T_ARG + (1 - t) * P
                    for h in range(2):
                        mm = t_.matmul(ps[:, 4 + h, :], log, tf[:, col + h * N:col + h * N + N], start=True, stop=True)
                    mm.then_inc(s_arg, 1)

                def scores(r):
                    i, j = ROUNDS[r]
                    kind, n, t = ARGS[i]
                    at = rows_of(kind, j)
                    pe.wait_ge(s_qe, NA * l + i + 1)
                    pe.wait_ge(s_ke, NA * l + i + 1)
                    if r > 0:
                        pe.wait_ge(s_mask, NR * l + r)
                    else:
                        pe.wait_ge(s_pt, 4 * l + 4)
                        pe.wait_ge(s_soe, 4 * l + 4)
                    kv = k_buf.rearrange("p (v n) -> p v n", n=P)
                    qv = q_buf.rearrange("p (v n) -> p v n", n=P)
                    for v in range(N_LEVELS):
                        t_.matmul(banks(6, 2)[:, v * P:v * P + P], kv[at, t + v, :], qv[at, t + v, :], start=True, stop=True)
                    mm = t_.matmul(banks(6, 2)[:, 7 * P:8 * P], k_block(kind, n, t)[at, :], q_block(kind, n, t)[at, :],
                                   start=True, stop=True)
                    if t == 1:
                        if cross_before(r) > 0:
                            pe.wait_ge(s_px, NX * l + cross_before(r))
                        mm = t_.matmul(banks(2)[:, 0:P], k_cross[at, :], qv[at, 0, :], start=True, stop=True)
                    mm.then_inc(s_sc, 1)

                def out_of(r):
                    i, j = ROUNDS[r]
                    kind, n, t = ARGS[i]
                    head = 2 * n + j if kind == "G" else n
                    val = v_g if kind == "G" else v_h
                    pe.wait_ge(s_psum, NR * l + r + 1)
                    if r > 0:
                        pe.wait_ge(s_oe, NR * l + r)
                    dst = banks(3)[:, (r % 2) * P:(r % 2) * P + P]
                    mm = t_.matmul(dst, p_sum[:, (r % 2) * P:(r % 2) * P + P], val[:, t * N + head * P:t * N + head * P + P],
                                   start=True, stop=t == 0)
                    if t == 1:
                        pe.wait_ge(s_px, NX * l + cross_before(r) + 1)
                        mm = t_.matmul(dst, p_cross, val[:, head * P:head * P + P], start=False, stop=True)
                    mm.then_inc(s_o, 1)

                args(0)
                for i in range(NA):
                    if i >= 8 and i + 1 < NA:
                        args(i + 1)
                    for r in [r for r, (q, _) in enumerate(ROUNDS) if q == i]:
                        scores(r)
                        if i < 8 and ROUNDS[r][1] == 0:
                            args(i + 1)
                        if r > 0:
                            out_of(r - 1)
                    if i < 8:
                        merge(4 + i)
                out_of(NR - 1)

                def branch(bi):
                    b = BRANCHES[bi]
                    src = [o_a, o_b, o_c][b]
                    if b != 1:
                        pe.wait_ge(s_heads, 2 * l + (1 if b == 0 else 2))
                    stage_groups(g_layer + 15 + 2 * bi, src)

                def branch_product(bi):
                    pe.wait_ge(s_free, g_layer - 1 + 15 + 2 * bi + 2)
                    for n in range(2):
                        c = 15 + 2 * bi + n
                        if c == 15:
                            pe.wait_ge(s_eva, 30 * l + 30)
                            pe.wait_ge(s_oe, NR * l + NR)
                        elif bi > 0:
                            pe.wait_ge(s_evd, 12 * l + 2 * (2 * (bi - 1) + n + 1))
                        left = lambda k, t: (x_hi[:, (bi % 2) * 1024 + k * SEQ + t * P:(bi % 2) * 1024 + k * SEQ + t * P + P],
                                             x_lo[:, (bi % 2) * 1024 + k * SEQ + t * P:(bi % 2) * 1024 + k * SEQ + t * P + P])
                        product(pe, Unit(base + 30 + 2 * bi + n), left, [ps[:, pair(c) + t, :] for t in range(NT)], N,
                                True, True, 0)

                branch(0)
                branch(1)
                branch_product(0)
                branch(2)
                branch_product(1)
                branch_product(2)
                for i in range(4):
                    pe.wait_ge(s_merged, 4 * l + (2 if i < 2 else 4))
                    turn_group(g_layer + 21 + i, [merged[:, t * D + k * P:t * D + k * P + P] for k in (2 * i, 2 * i + 1)
                                                  for t in range(NT)])
                for n in range(2):
                    acc = [ps[:, 2 * n + t, :] for t in range(NT)]
                    pe.wait_ge(s_free, g_layer - 1 + 23 + 2 * n)
                    product(pe, Unit(base + 36 + 2 * n), model_left, acc, N, True, False, 0)
                    pe.wait_ge(s_free, g_layer - 1 + 25)
                    product(pe, Unit(base + 37 + 2 * n), model_left, acc, N, False, True, 4)
                norm_groups(2 * l + 1, g_layer + 25)
                pe.wait_ge(s_free, g_layer - 1 + 29)
                if l == 0:
                    ff(U_FFN, 0, 0, FFN_STEPS, NT, model_left, mod_steps=8)
                    pe.wait_ge(s_xupd, 2 * NT)

            pe.wait_ge(s_rsp, 2)
            for k in range(KD):
                hi, lo = x_hi[:, k * SEQ:k * SEQ + SEQ], x_lo[:, k * SEQ:k * SEQ + SEQ]
                for i, (lhs, rhs) in enumerate(((r_hi, hi), (r_lo, hi), (r_hi, lo), (r_lo, lo))):
                    mm = t_.matmul(banks(6)[0:N_EXP, 0:SEQ], lhs[:, k * 8:k * 8 + 8], rhs,
                                   start=k == 0 and i == 0, stop=k == KD - 1 and i == 3)
            mm.then_inc(s_logit, 1)
            pe.wait_ge(s_lrow, 1)
            for t in range(NT):
                mm = t_.transpose(banks(7)[:, t * 8:t * 8 + 8], logit_rows[:, t * P:t * P + P],
                                  ident[0:N_EXP, 0:N_EXP])
            mm.then_inc(s_logit, 1)
            pe.wait_ge(s_m, 1)
            tri, one = tb[:, B_TRI:B_TRI + P], tb[:, B_ONES:B_ONES + P]
            m0, m1 = m_bf[:, 0:8], m_bf[:, 8:16]
            t_.matmul(banks(7)[:, 0:8], tri, m0, start=True, stop=True)
            t_.matmul(banks(7)[:, 8:16], one, m0, start=True, stop=False)
            t_.matmul(banks(7)[:, 8:16], tri, m1, start=False, stop=True)
            t_.matmul(banks(7)[:, 16:24], one, m0, start=True, stop=False)
            t_.matmul(banks(7)[:, 16:24], one, m1, start=False, stop=True).then_inc(s_pos, 1)

            def gather(n, half):
                pe.wait_ge(s_sel, n)
                for k in range(4 * half, 4 * half + 4):
                    for t in range(NT):
                        mm = t_.matmul(banks(6, 2)[:, k * P:k * P + P], xhat[:, t * D + k * P:t * D + k * P + P],
                                       sel[:, t * P:t * P + P], start=t == 0, stop=t == NT - 1)
                if half:
                    mm.then_inc(s_gat, 1)

            def item_left(k, t):
                return x_hi[:, k * P:k * P + P], x_lo[:, k * P:k * P + P]

            gather(1, 0)
            gather(1, 1)
            pe.wait_ge(s_ids, 1)
            items = pe.value_load(ids[0:1, 0:1], min_val=0, max_val=MAX_OVER) + N_EXP
            for h in range(2):
                mm = t_.matmul(ps[:, 4 + h, :], tb[:, B_ZERO:B_ZERO + P], tb[:, B_MASK:B_MASK + N], start=True, stop=True)
            mm.then_inc(s_yzero, 1)

            def scatter(n, t, bank):
                for h in range(2):
                    mm = t_.matmul(ps[:, bank + h, :], sel_t[:, t * P:t * P + P], y_sb[:, h * N:h * N + N],
                                   start=True, stop=True)
                mm.then_inc(s_scat, 1)

            with pe.Fori(0, items) as it:
                def first():
                    pe.wait_ge(s_ysb, it + 1)
                    pe.wait_ge(s_selc, it + 1)
                    scatter(it, 0, 6)

                def second():
                    pe.wait_ge(s_yadd, 2 * it + 1)
                    scatter(it, 1, 6)

                def third():
                    pe.wait_ge(s_selw, it + 1)
                    for t in range(NT):
                        mm = t_.transpose(banks(3)[:, t * P:t * P + P], sel_w[:, t * P:t * P + P], ident)
                    mm.then_inc(s_selt, 1)
                    pe.wait_ge(s_yadd, 2 * it + 2)
                    gather(it + 2, 0)

                pe.wait_ge(s_hglo, it + 1)
                ff(U_MOE, it * MOE_STEPS, it * MOE_STEPS + FFN_STEPS, MOE_STEPS, 1, item_left, first=first,
                   early=(None, second, third, lambda: gather(it + 2, 1), None))
            pe.wait_ge(s_ysb, items + 1)
            pe.wait_ge(s_selc, items + 1)
            scatter(items, 0, 6)
            scatter(items, 1, 4)


_INS = ['x', 'c', 'w_mod', 'b_mod', 'norm_g', 'w_in', 'gla_w_gate', 'gla_b_gate', 'gla_norm_g', 'swa_sinks', 'hgrn_lb',
        'hgrn_norm_g', 'w_branch', 'w_merge', 'b_merge', 'w_out', 'ffn_w_gate', 'ffn_w_up', 'ffn_w_down', 'moe_router',
        'moe_w_gate', 'moe_w_up', 'moe_w_down']


def shape_tables():
    import numpy as np

    s, t = np.arange(P)[:, None], np.arange(P)[None, :]
    args, masks = [], []
    for v in range(N_LEVELS):
        half = P >> (v + 1)
        mid = t // (2 * half) * (2 * half) + half - 1
        args.append(np.where(t > mid, (s > mid) & (s <= t), (s > t) & (s <= mid)))
        same = s // (2 * half) == t // (2 * half)
        masks.append(same & (t > mid) & (s <= mid))
    prefix, suffix = s <= t, s > t
    f32 = np.concatenate([np.eye(P, dtype=bool), prefix] + args + [suffix], axis=1).astype(np.float32)
    chunk = 64

    def dist(q0, n):
        q, k = q0 + np.arange(P)[:, None], np.arange(n)[None, :]
        seen = (k // chunk <= q // chunk) & (k // chunk >= q // chunk - 1)
        return np.where(seen, np.abs(q - k), NEVER)

    zero = np.zeros((P, P))
    bf = np.concatenate([np.concatenate(masks + [s == t], axis=1).astype(np.float64), dist(0, P), dist(P, 2 * P),
                         (s < t).astype(np.float64), np.broadcast_to(t, (P, P)).astype(np.float64), zero + 1, zero], axis=1)
    return {"table_f32": f32, "table_bf16": bf.astype(mybir.dt.np(BF16)), "ones_row": np.ones((1, SEQ), np.float32)}


def kernel(**inputs):
    import numpy as _np
    import concourse.bacc as _bacc
    from concourse import mybir as _mybir
    from concourse.bass_utils import run_bass_kernel_spmd as _run

    nc = _bacc.Bacc("TRN2", target_bir_lowering=False, num_devices=1)
    arrays, args = {}, {}
    given = {name: _np.ascontiguousarray(inputs[name]) for name in _INS}
    given.update(shape_tables())
    for name, arr in given.items():
        arrays[f"in_{name}_dram"] = arr
        args[name] = nc.dram_tensor(f"in_{name}_dram", arr.shape, _mybir.dt.from_np(arr.dtype),
                                    kind="ExternalInput").ap()
    out = nc.dram_tensor("out_0_dram", (1, SEQ, D), _mybir.dt.float32, kind="ExternalOutput").ap()
    program(nc, args, out)
    r = _run(nc, [arrays], core_ids=[0])
    return r.results[0]["out_0_dram"]
```
